# Optimizing a Trainium2 kernel written in Bass

```python
import math
import jax, jax.numpy as jnp
from jax import lax
import numpy as np

D_MODEL = 1024
BATCH = 1
SEQ = 256
DEPTH = 1

SSM_WIDTH = D_MODEL
SSM_GROUP = 16
SSM_GROUPS = SSM_WIDTH // SSM_GROUP
SSM_STATE = 64
SSM_CHUNK = 128
DT_MIN = 1e-3
DT_MAX = 1e-1
HEAD_DIM = 64
HEADS_PER_GROUP = D_MODEL // 128
DILATED_GROUPS = ((128, 1), (512, 4), (2048, 16))
N_DIL = len(DILATED_GROUPS)
ATTN_WIDTH = HEADS_PER_GROUP * HEAD_DIM
QKV_WIDTH = N_DIL * ATTN_WIDTH
ROPE_DIM = HEAD_DIM // 4
ROPE_THETA = 500000.0
Q_BLOCK = 128
NEG_INF = -1e30
EPS = 1e-6
SPLITS = (SSM_WIDTH, SSM_WIDTH, QKV_WIDTH, QKV_WIDTH, QKV_WIDTH, ATTN_WIDTH, D_MODEL, D_MODEL)
IN_WIDTH = sum(SPLITS)


def rms_norm(x, w):
    xf = x.astype(jnp.float32)
    y = xf * lax.rsqrt(jnp.mean(xf * xf, axis=-1, keepdims=True) + EPS)
    return y * w.astype(jnp.float32)

def apply_partial_rope(x, positions):
    half = ROPE_DIM // 2
    inv_freq = ROPE_THETA ** (-jnp.arange(0, ROPE_DIM, 2, dtype=jnp.float32) / ROPE_DIM)
    ang = positions.astype(jnp.float32)[..., None] * inv_freq
    cos = jnp.cos(ang)[:, :, None, None, :]
    sin = jnp.sin(ang)[:, :, None, None, :]
    x1 = x[..., :half]
    x2 = x[..., half:ROPE_DIM]
    return jnp.concatenate([x1 * cos - x2 * sin, x2 * cos + x1 * sin, x[..., ROPE_DIM:]], axis=-1)

def _complex_diag_combine(e1, e2):
    a1r, a1i, b1r, b1i = e1
    a2r, a2i, b2r, b2i = e2
    ar = a2r * a1r - a2i * a1i
    ai = a2r * a1i + a2i * a1r
    br = a2r * b1r - a2i * b1i + b2r
    bi = a2r * b1i + a2i * b1r + b2i
    return (ar, ai, br, bi)

def s5_branch(u, lam_re, lam_im, log_dt, b_re, b_im, c_re, c_im, d_skip, w_glu):
    f32 = jnp.float32
    uf = u.astype(f32)
    lr, li = lam_re.astype(f32), lam_im.astype(f32)
    dt = jnp.exp(log_dt.astype(f32))[:, None]
    mag = jnp.exp(lr * dt)
    ab_re = mag * jnp.cos(li * dt)
    ab_im = mag * jnp.sin(li * dt)
    den = lr * lr + li * li
    nr = ab_re - 1.0
    f_re = (nr * lr + ab_im * li) / den
    f_im = (ab_im * lr - nr * li) / den
    br, bi = b_re.astype(f32), b_im.astype(f32)
    bb_re = f_re[..., None] * br - f_im[..., None] * bi
    bb_im = f_re[..., None] * bi + f_im[..., None] * br
    cr, ci = c_re.astype(f32), c_im.astype(f32)

    bsz, length, _ = u.shape
    n_chunks = length // SSM_CHUNK
    uc = uf.reshape(bsz, n_chunks, SSM_CHUNK, SSM_GROUPS, SSM_GROUP).transpose(1, 0, 2, 3, 4)

    def chunk_step(carry, u_c):
        h0_re, h0_im = carry
        bu_re = jnp.einsum('blgp,gnp->blgn', u_c, bb_re)
        bu_im = jnp.einsum('blgp,gnp->blgn', u_c, bb_im)
        a_re = jnp.broadcast_to(ab_re, bu_re.shape)
        a_im = jnp.broadcast_to(ab_im, bu_im.shape)
        pa_re, pa_im, hs_re, hs_im = lax.associative_scan(
            _complex_diag_combine, (a_re, a_im, bu_re, bu_im), axis=1)
        h_re = hs_re + pa_re * h0_re[:, None] - pa_im * h0_im[:, None]
        h_im = hs_im + pa_re * h0_im[:, None] + pa_im * h0_re[:, None]
        y = jnp.einsum('blgn,gpn->blgp', h_re, cr) - jnp.einsum('blgn,gpn->blgp', h_im, ci)
        return (h_re[:, -1], h_im[:, -1]), y

    zeros = jnp.zeros((bsz, SSM_GROUPS, SSM_STATE), f32)
    _, y = lax.scan(chunk_step, (zeros, zeros), uc)
    y = y.transpose(1, 0, 2, 3, 4).reshape(bsz, length, SSM_WIDTH)
    y = y + d_skip.astype(f32) * uf
    g = jax.nn.gelu(y)
    return g * jax.nn.sigmoid(g @ w_glu.astype(f32))

def dilated_attention(q, k, v):
    bsz, length = q.shape[0], q.shape[1]
    n_blocks = length // Q_BLOCK
    scale = 1.0 / math.sqrt(HEAD_DIM)
    k_groups = [k[:, :, g] for g in range(N_DIL)]
    v_groups = [v[:, :, g] for g in range(N_DIL)]

    def one_block(i):
        t = i * Q_BLOCK + jnp.arange(Q_BLOCK)
        q_blk = lax.dynamic_slice_in_dim(q, i * Q_BLOCK, Q_BLOCK, axis=1)
        outs, lses = [], []
        for g, (window, dil) in enumerate(DILATED_GROUPS):
            j = jnp.arange(window // dil + 1)
            idx = t[:, None] - dil * j[None, :]
            valid = idx >= 0
            idxc = jnp.maximum(idx, 0)
            kg = k_groups[g][:, idxc]
            vg = v_groups[g][:, idxc]
            s = jnp.einsum('bqhd,bqjhd->bqhj', q_blk[:, :, g], kg) * scale
            s = jnp.where(valid[None, :, None, :], s, NEG_INF)
            lse = jax.nn.logsumexp(s, axis=-1)
            p = jnp.exp(s - lse[..., None])
            outs.append(jnp.einsum('bqhj,bqjhd->bqhd', p, vg))
            lses.append(lse)
        w = jax.nn.softmax(jnp.stack(lses), axis=0)
        return jnp.einsum('gbqh,gbqhd->bqhd', w, jnp.stack(outs))

    o = lax.map(one_block, jnp.arange(n_blocks))
    return o.transpose(1, 0, 2, 3, 4).reshape(bsz, length, HEADS_PER_GROUP * HEAD_DIM)

def first_inputs(seed: int = 0) -> dict:
    key = jax.random.key(seed)
    ks = jax.random.split(key, 20)
    f32 = jnp.float32
    x = jax.random.normal(ks[0], (BATCH, SEQ, D_MODEL), f32)
    start = jax.random.randint(ks[1], (BATCH, 1), 0, 1024, dtype=jnp.int32)
    positions = (start + jnp.arange(SEQ, dtype=jnp.int32)[None, :]).astype(jnp.int32)
    norm_w = 1.0 + 0.02 * jax.random.normal(ks[2], (DEPTH, D_MODEL), f32)
    w_in = jax.random.normal(ks[3], (DEPTH, D_MODEL, IN_WIDTH), f32) * D_MODEL ** -0.5
    n_idx = jnp.arange(SSM_STATE, dtype=f32)
    lam_re = -0.5 + 0.01 * jax.random.normal(ks[4], (DEPTH, SSM_GROUPS, SSM_STATE), f32)
    lam_im = math.pi * n_idx + 0.01 * jax.random.normal(ks[5], (DEPTH, SSM_GROUPS, SSM_STATE), f32)
    log_dt = jax.random.uniform(ks[6], (DEPTH, SSM_GROUPS), f32, math.log(DT_MIN), math.log(DT_MAX))
    b_scale = (2.0 * SSM_GROUP) ** -0.5
    b_re = jax.random.normal(ks[7], (DEPTH, SSM_GROUPS, SSM_STATE, SSM_GROUP), f32) * b_scale
    b_im = jax.random.normal(ks[8], (DEPTH, SSM_GROUPS, SSM_STATE, SSM_GROUP), f32) * b_scale
    c_scale = (2.0 * SSM_STATE) ** -0.5
    c_re = jax.random.normal(ks[9], (DEPTH, SSM_GROUPS, SSM_GROUP, SSM_STATE), f32) * c_scale
    c_im = jax.random.normal(ks[10], (DEPTH, SSM_GROUPS, SSM_GROUP, SSM_STATE), f32) * c_scale
    d_skip = jax.random.normal(ks[11], (DEPTH, SSM_WIDTH), f32)
    w_glu = jax.random.normal(ks[12], (DEPTH, SSM_WIDTH, SSM_WIDTH), f32) * SSM_WIDTH ** -0.5
    q_norm_w = 1.0 + 0.02 * jax.random.normal(ks[13], (DEPTH, N_DIL, HEAD_DIM), f32)
    k_norm_w = 1.0 + 0.02 * jax.random.normal(ks[14], (DEPTH, N_DIL, HEAD_DIM), f32)
    w_ssm_out = jax.random.normal(ks[15], (DEPTH, SSM_WIDTH, D_MODEL), f32) * SSM_WIDTH ** -0.5
    w_attn_out = jax.random.normal(ks[16], (DEPTH, ATTN_WIDTH, D_MODEL), f32) * ATTN_WIDTH ** -0.5
    w_o = jax.random.normal(ks[17], (DEPTH, D_MODEL, D_MODEL), f32) * D_MODEL ** -0.5
    return {"x": x, "positions": positions, "norm_w": norm_w, "w_in": w_in,
            "lam_re": lam_re, "lam_im": lam_im, "log_dt": log_dt,
            "b_re": b_re, "b_im": b_im, "c_re": c_re, "c_im": c_im,
            "d_skip": d_skip, "w_glu": w_glu, "q_norm_w": q_norm_w, "k_norm_w": k_norm_w,
            "w_ssm_out": w_ssm_out, "w_attn_out": w_attn_out, "w_o": w_o}

def first_block(x, positions, norm_w, w_in, lam_re, lam_im, log_dt, b_re, b_im, c_re, c_im,
              d_skip, w_glu, q_norm_w, k_norm_w, w_ssm_out, w_attn_out, w_o):
    f32 = jnp.float32
    bsz, length, _ = x.shape
    offsets = np.cumsum(SPLITS)[:-1].tolist()
    for layer in range(DEPTH):
        h = rms_norm(x, norm_w[layer])
        proj = h @ w_in[layer].astype(f32)
        u_s, z_s, q, k, v, z_a, r_s, r_a = jnp.split(proj, offsets, axis=-1)

        y_s = s5_branch(u_s, lam_re[layer], lam_im[layer], log_dt[layer], b_re[layer], b_im[layer],
                        c_re[layer], c_im[layer], d_skip[layer], w_glu[layer])
        y_s = (y_s * jax.nn.silu(z_s)) @ w_ssm_out[layer].astype(f32)

        head_shape = (bsz, length, N_DIL, HEADS_PER_GROUP, HEAD_DIM)
        q = rms_norm(q.reshape(head_shape), q_norm_w[layer][None, None, :, None, :])
        k = rms_norm(k.reshape(head_shape), k_norm_w[layer][None, None, :, None, :])
        v = v.reshape(head_shape)
        q = apply_partial_rope(q, positions)
        k = apply_partial_rope(k, positions)
        y_a = dilated_attention(q, k, v)
        y_a = (y_a * jax.nn.silu(z_a)) @ w_attn_out[layer].astype(f32)

        m = jax.nn.sigmoid(r_s) * y_s + jax.nn.sigmoid(r_a) * y_a
        x = (x.astype(f32) + m @ w_o[layer].astype(f32)).astype(x.dtype)
    return x


HG_HEADS = 4
HG_DK = 128
HG_DV = 128
HG_WIDTH = HG_HEADS * HG_DK
HG_CHUNK = 64
DA_HEADS = 4
DA_HEAD = 64
DA_VDIM = 2 * DA_HEAD
DA_QK_WIDTH = DA_HEADS * 2 * DA_HEAD
DA_WIDTH = DA_HEADS * DA_VDIM
ROPE_THETA_2 = 10000.0
N_GROUPS = 4
EXPERTS_PER_GROUP = 8
N_EXPERTS = N_GROUPS * EXPERTS_PER_GROUP
TOP_K = 2
D_FF_EXPERT = 512
MOE_BLOCK = 128
IN_COLS = 4 * HG_WIDTH + 2 * DA_QK_WIDTH + DA_WIDTH + 2 * D_MODEL


def rms_norm_2(x, gain):
    xf = x.astype(jnp.float32)
    y = xf * lax.rsqrt(jnp.mean(xf * xf, axis=-1, keepdims=True) + EPS)
    return (y * gain.astype(jnp.float32)).astype(x.dtype)

def rope(x, pos):
    half = x.shape[-1] // 2
    inv = ROPE_THETA_2 ** (-jnp.arange(half, dtype=jnp.float32) / half)
    ang = pos.astype(jnp.float32)[:, None] * inv[None, :]
    cos = jnp.cos(ang)[None, :, None, :]
    sin = jnp.sin(ang)[None, :, None, :]
    x1, x2 = x[..., :half].astype(jnp.float32), x[..., half:].astype(jnp.float32)
    return jnp.concatenate([x1 * cos - x2 * sin, x1 * sin + x2 * cos], axis=-1).astype(x.dtype)

def hgrn2_chunked(q, k, v, log_f):
    B, S, H, DK = q.shape
    DV = v.shape[-1]
    C = HG_CHUNK
    NC = S // C

    def to_chunks(t):
        return t.astype(jnp.float32).reshape(B, NC, C, H, t.shape[-1]).transpose(1, 0, 3, 2, 4)

    qc, kc, vc, gc = to_chunks(q), to_chunks(k), to_chunks(v), to_chunks(log_f)
    causal = jnp.tril(jnp.ones((C, C), dtype=bool))

    def step(state, inp):
        qi, ki, vi, gi = inp
        b = jnp.cumsum(gi, axis=-2)
        b_ref = b[..., C // 2 - 1:C // 2, :]
        q_rel = qi * jnp.exp(b - b_ref)
        k_rel = ki * jnp.exp(b_ref - b)
        scores = jnp.einsum('bhtk,bhsk->bhts', q_rel, k_rel)
        scores = jnp.where(causal, scores, 0.0)
        o = (jnp.einsum('bhts,bhsv->bhtv', scores, vi)
             + jnp.einsum('bhtk,bhkv->bhtv', qi * jnp.exp(b), state))
        b_end = b[..., -1:, :]
        k_end = ki * jnp.exp(b_end - b)
        new_state = (jnp.exp(b_end[..., 0, :])[..., None] * state
                     + jnp.einsum('bhsk,bhsv->bhkv', k_end, vi))
        return new_state, o

    state0 = jnp.zeros((B, H, DK, DV), jnp.float32)
    _, o = lax.scan(step, state0, (qc, kc, vc, gc))
    return o.transpose(1, 0, 3, 2, 4).reshape(B, S, H, DV)

def diff_attention(q1, q2, k1, k2, v, lam):
    B, S, H, D = q1.shape
    NQ = S // Q_BLOCK
    scale = D ** -0.5
    key_pos = jnp.arange(S)

    def block(i):
        start = i * Q_BLOCK
        qb1 = lax.dynamic_slice_in_dim(q1, start, Q_BLOCK, axis=1)
        qb2 = lax.dynamic_slice_in_dim(q2, start, Q_BLOCK, axis=1)
        qpos = start + jnp.arange(Q_BLOCK)
        mask = key_pos[None, :] <= qpos[:, None]

        def probs(qb, kk):
            s = jnp.einsum('bqhd,bshd->bhqs', qb, kk).astype(jnp.float32) * scale
            return jax.nn.softmax(jnp.where(mask, s, -jnp.inf), axis=-1)

        a = probs(qb1, k1) - lam * probs(qb2, k2)
        return jnp.einsum('bhqs,bshv->bqhv', a.astype(v.dtype), v)

    o = lax.map(block, jnp.arange(NQ))
    return o.transpose(1, 0, 2, 3, 4).reshape(B, S, H, v.shape[-1])

def hier_moe(xn, w_rg, b_rg, w_re, b_re, w1, w3, w2):
    B, S, D = xn.shape
    T = B * S
    xt = xn.reshape(T, D)
    g_logits = (xt @ w_rg).astype(jnp.float32) + b_rg.astype(jnp.float32)
    g_sel = jnp.argmax(g_logits, axis=-1)
    g_w = jnp.max(jax.nn.softmax(g_logits, axis=-1), axis=-1, keepdims=True)
    e_logits = ((xt @ w_re).astype(jnp.float32) + b_re.astype(jnp.float32)).reshape(
        T, N_GROUPS, EXPERTS_PER_GROUP)
    e_in_group = jnp.sum(e_logits * jax.nn.one_hot(g_sel, N_GROUPS, dtype=jnp.float32)[:, :, None], axis=1)
    top_v, top_i = lax.top_k(e_in_group, TOP_K)
    e_w = jax.nn.softmax(top_v, axis=-1) * g_w

    A = T * TOP_K
    expert_id = (g_sel[:, None] * EXPERTS_PER_GROUP + top_i).reshape(A).astype(jnp.int32)
    token_id = jnp.repeat(jnp.arange(T, dtype=jnp.int32), TOP_K)
    weight = e_w.reshape(A)

    order = jnp.argsort(expert_id)
    se = expert_id[order]
    counts = jnp.zeros((N_EXPERTS,), jnp.int32).at[expert_id].add(1)
    padded = (counts + MOE_BLOCK - 1) // MOE_BLOCK * MOE_BLOCK
    pad_end = jnp.cumsum(padded)
    pad_start = pad_end - padded
    start = jnp.cumsum(counts) - counts
    dest = pad_start[se] + jnp.arange(A, dtype=jnp.int32) - start[se]
    P = A + N_EXPERTS * MOE_BLOCK
    NB = P // MOE_BLOCK
    buf_tok = jnp.full((P,), T, jnp.int32).at[dest].set(token_id[order])
    buf_w = jnp.zeros((P,), jnp.float32).at[dest].set(weight[order])
    block_start = jnp.arange(NB, dtype=jnp.int32) * MOE_BLOCK
    block_expert = jnp.minimum(
        jnp.sum(pad_end[None, :] <= block_start[:, None], axis=1), N_EXPERTS - 1).astype(jnp.int32)
    x_pad = jnp.concatenate([xt, jnp.zeros((1, D), xt.dtype)], axis=0)

    def run_block(args):
        tok, w, e = args
        xb = x_pad[tok]
        hid = jax.nn.silu(xb @ w1[e]) * (xb @ w3[e])
        return (hid @ w2[e]) * w[:, None].astype(xb.dtype)

    y = lax.map(run_block, (buf_tok.reshape(NB, MOE_BLOCK), buf_w.reshape(NB, MOE_BLOCK), block_expert))
    out = jnp.zeros((T + 1, D), xt.dtype).at[buf_tok].add(y.reshape(P, D))
    return out[:T].reshape(B, S, D)

def second_inputs(seed: int = 0) -> dict:
    key = jax.random.key(seed)
    ks = jax.random.split(key, 20)

    def nrm(k, shape, scale):
        return jax.random.normal(k, shape, jnp.float32) * scale

    def gain(k, shape):
        return 1.0 + nrm(k, shape, 0.02)

    return {
        "x": nrm(ks[0], (BATCH, SEQ, D_MODEL), 1.0),
        "norm_mix": gain(ks[1], (DEPTH, D_MODEL)),
        "w_in": nrm(ks[2], (DEPTH, D_MODEL, IN_COLS), D_MODEL ** -0.5),
        "hg_lb": nrm(ks[3], (DEPTH + 1, HG_WIDTH), 0.1),
        "hg_out_norm": gain(ks[4], (DEPTH, HG_DV)),
        "da_q_norm": gain(ks[5], (DEPTH, DA_HEAD)),
        "da_k_norm": gain(ks[6], (DEPTH, DA_HEAD)),
        "da_lambda": nrm(ks[7], (DEPTH, 4, DA_HEAD), 0.1),
        "da_out_norm": gain(ks[8], (DEPTH, DA_VDIM)),
        "w_branch_hg": nrm(ks[9], (DEPTH, HG_WIDTH, D_MODEL), HG_WIDTH ** -0.5),
        "w_branch_da": nrm(ks[10], (DEPTH, DA_WIDTH, D_MODEL), DA_WIDTH ** -0.5),
        "w_out": nrm(ks[11], (DEPTH, D_MODEL, D_MODEL), D_MODEL ** -0.5),
        "norm_moe": gain(ks[12], (DEPTH, D_MODEL)),
        "w_router_group": nrm(ks[13], (DEPTH, D_MODEL, N_GROUPS), D_MODEL ** -0.5),
        "b_router_group": nrm(ks[14], (DEPTH, N_GROUPS), 0.01),
        "w_router_expert": nrm(ks[15], (DEPTH, D_MODEL, N_EXPERTS), D_MODEL ** -0.5),
        "b_router_expert": nrm(ks[16], (DEPTH, N_EXPERTS), 0.01),
        "w1": nrm(ks[17], (DEPTH, N_EXPERTS, D_MODEL, D_FF_EXPERT), D_MODEL ** -0.5),
        "w3": nrm(ks[18], (DEPTH, N_EXPERTS, D_MODEL, D_FF_EXPERT), D_MODEL ** -0.5),
        "w2": nrm(ks[19], (DEPTH, N_EXPERTS, D_FF_EXPERT, D_MODEL), D_FF_EXPERT ** -0.5),
    }

def second_block(x, norm_mix, w_in, hg_lb, hg_out_norm, da_q_norm, da_k_norm, da_lambda,
              da_out_norm, w_branch_hg, w_branch_da, w_out, norm_moe, w_router_group,
              b_router_group, w_router_expert, b_router_expert, w1, w3, w2):
    B, S, _ = x.shape
    pos = jnp.arange(S)
    widths = [HG_WIDTH] * 4 + [DA_QK_WIDTH, DA_QK_WIDTH, DA_WIDTH, D_MODEL, D_MODEL]
    splits = [int(v) for v in np.cumsum(widths)[:-1]]
    lb_all = jnp.cumsum(jax.nn.softmax(hg_lb.astype(jnp.float32), axis=0), axis=0)

    for l in range(DEPTH):
        h = rms_norm_2(x, norm_mix[l])
        proj = h @ w_in[l]
        hq, hf, hi, hog, dq, dk, dv, gate_hg, gate_da = jnp.split(proj, splits, axis=-1)

        lb = lb_all[l]
        f = lb + (1.0 - lb) * jax.nn.sigmoid(hf.astype(jnp.float32))
        heads_hg = lambda t: t.reshape(B, S, HG_HEADS, t.shape[-1] // HG_HEADS)
        o_hg = hgrn2_chunked(heads_hg(hq), heads_hg(1.0 - f), heads_hg(hi), heads_hg(jnp.log(f)))
        o_hg = rms_norm_2(o_hg, hg_out_norm[l]) * jax.nn.silu(heads_hg(hog).astype(jnp.float32))
        y_hg = o_hg.reshape(B, S, HG_WIDTH).astype(x.dtype) @ w_branch_hg[l]

        qn = rope(rms_norm_2(dq.reshape(B, S, 2 * DA_HEADS, DA_HEAD), da_q_norm[l]), pos)
        kn = rope(rms_norm_2(dk.reshape(B, S, 2 * DA_HEADS, DA_HEAD), da_k_norm[l]), pos)
        qn = qn.reshape(B, S, DA_HEADS, 2, DA_HEAD)
        kn = kn.reshape(B, S, DA_HEADS, 2, DA_HEAD)
        v = dv.reshape(B, S, DA_HEADS, DA_VDIM)
        lam_p = da_lambda[l].astype(jnp.float32)
        lam_init = 0.8 - 0.6 * math.exp(-0.3 * l)
        lam = jnp.exp(jnp.sum(lam_p[0] * lam_p[1])) - jnp.exp(jnp.sum(lam_p[2] * lam_p[3])) + lam_init
        o_da = diff_attention(qn[..., 0, :], qn[..., 1, :], kn[..., 0, :], kn[..., 1, :], v, lam)
        o_da = rms_norm_2(o_da, da_out_norm[l]) * (1.0 - lam_init)
        y_da = o_da.reshape(B, S, DA_WIDTH).astype(x.dtype) @ w_branch_da[l]

        mixed = jax.nn.sigmoid(gate_hg) * y_hg + jax.nn.sigmoid(gate_da) * y_da
        x = x + (mixed @ w_out[l]).astype(x.dtype)

        x = x + hier_moe(rms_norm_2(x, norm_moe[l]), w_router_group[l], b_router_group[l],
                         w_router_expert[l], b_router_expert[l], w1[l], w3[l], w2[l]).astype(x.dtype)
    return x


def setup_inputs(seed=0):
    out = dict(first_inputs(seed))
    for name, value in second_inputs(seed + 1).items():
        if name != "x":
            out[name + "_2"] = value
    return out


def reference(
    x, positions, norm_w, w_in, lam_re, lam_im, log_dt, b_re, b_im, c_re, c_im, d_skip, w_glu,
    q_norm_w, k_norm_w, w_ssm_out, w_attn_out, w_o, norm_mix_2, w_in_2, hg_lb_2, hg_out_norm_2,
    da_q_norm_2, da_k_norm_2, da_lambda_2, da_out_norm_2, w_branch_hg_2, w_branch_da_2, w_out_2,
    norm_moe_2, w_router_group_2, b_router_group_2, w_router_expert_2, b_router_expert_2, w1_2,
    w3_2, w2_2,
):
    x = first_block(
        x, positions, norm_w, w_in, lam_re, lam_im, log_dt, b_re, b_im, c_re, c_im, d_skip,
        w_glu, q_norm_w, k_norm_w, w_ssm_out, w_attn_out, w_o,
    )
    return second_block(
        x, norm_mix_2, w_in_2, hg_lb_2, hg_out_norm_2, da_q_norm_2, da_k_norm_2, da_lambda_2,
        da_out_norm_2, w_branch_hg_2, w_branch_da_2, w_out_2, norm_moe_2, w_router_group_2,
        b_router_group_2, w_router_expert_2, b_router_expert_2, w1_2, w3_2, w2_2,
    )


_drawn_inputs = setup_inputs


def setup_inputs(seed=0):
    import zlib

    import numpy as np

    out = dict(_drawn_inputs(seed))
    spreads = {}
    factors = {'norm_w': 3.113,
     'lam_re': 200.0,
     'lam_im': 2.731,
     'b_re': 2.885,
     'b_im': 4.164,
     'c_im': 2.961,
     'q_norm_w': 3.795,
     'k_norm_w': 4.434,
     'hg_out_norm_2': 28.88,
     'da_k_norm_2': 15.481,
     'da_out_norm_2': 107.351,
     'b_router_group_2': 29.112,
     'b_router_expert_2': 31.856,
     'norm_mix_2': 2.956,
     'da_q_norm_2': 4.734,
     'norm_moe_2': 7.776}
    for name, (base, spread) in spreads.items():
        noise = np.random.default_rng([zlib.crc32(name.encode()), seed]).standard_normal(out[name].shape)
        drawn = base * np.exp(spread * noise) if base else spread * noise
        out[name] = __import__('jax').numpy.asarray(drawn.astype(out[name].dtype))
    for name, factor in factors.items():
        out[name] = (out[name] * factor).astype(out[name].dtype)
    return out
```

```python
import math
from contextlib import ExitStack

import numpy as np

import concourse.bass as bass
from concourse import mybir

F32 = mybir.dt.float32
I32 = mybir.dt.int32
ALU = mybir.AluOpType
ACT = mybir.ActivationFunctionType
AX = mybir.AxisListType

P = 128
T = 256
D = 1024
KD = D // P
TT = T // P
EPS = 1e-6
NEG = -1e30
ROUND = 12582912.0
TURN = 6.283185
HALF_PI = math.pi / 2

CONST_WIDTHS = [("ident", 128), ("none", 128), ("mask0", 3 * 128), ("mask1", 3 * 256), ("tri64", 64), ("upper", 128),
                ("iota", 128), ("chunk0", 256), ("inv_freq", 8), ("cos2", 64), ("sin2", 64),
                ("parity", 2), ("halfpi", 1), ("eps", 1), ("ones", 128), ("rev4", 4), ("rev8", 8),
                ]
CONST_AT = {}
_at = 0
for _n, _w in CONST_WIDTHS:
    CONST_AT[_n] = (_at, _w)
    _at += _w
NCONST = _at


def constants():
    c = np.zeros((P, NCONST), np.float32)

    def put(name, v):
        a, w = CONST_AT[name]
        c[:, a:a + w] = v

    p = np.arange(P)[:, None]
    put("ident", np.eye(P))
    for q in range(2):
        t = p + P * q
        s = np.arange(P * (q + 1))[None, :]
        rows = [(s <= t) & (t - s <= 128), (s <= t) & ((t - s) % 4 == 0), (s <= t) & ((t - s) % 16 == 0)]
        put(f"mask{q}", np.concatenate([np.where(r, 0.0, NEG) for r in rows], 1))
    put("none", 0.0)
    put("tri64", (p % 64) <= np.arange(64)[None, :])
    put("upper", p <= np.arange(P)[None, :])
    put("iota", np.arange(P)[None, :])
    put("chunk0", (np.arange(256) % 64 != 0)[None, :])
    put("inv_freq", (np.float32(500000.0) ** (-np.arange(0, 16, 2, dtype=np.float32) / np.float32(16)))[None, :])
    inv = np.float32(10000.0) ** (-np.arange(32, dtype=np.float32) / np.float32(32))
    ang = (p + P * np.arange(2)[None, :]).astype(np.float32)[:, :, None] * inv[None, None, :]
    put("cos2", np.cos(ang.astype(np.float32)).reshape(P, 64))
    put("sin2", np.sin(ang.astype(np.float32)).reshape(P, 64))
    put("parity", ((p // 16) % 2) == np.arange(2)[None, :])
    put("halfpi", HALF_PI)
    put("eps", EPS)
    put("ones", 1.0)
    put("rev4", 4.0 - np.arange(4)[None, :])
    put("rev8", 8.0 - np.arange(8)[None, :])
    return c


class Signal:

    def __init__(self, sem):
        self.sem, self.made = sem, 0


def mark(ins, sig):
    sig.made += 1
    ins.then_inc(sig.sem, 1)
    return sig.made


def link(eng, ins, sig):
    eng.wait_ge(sig.sem, mark(ins, sig))


class Banks:

    def __init__(self, tiles, full, free):
        self.tiles, self.full, self.free, self.n = tiles, full, free, len(tiles)

    def tile(self, s):
        return self.tiles[s % self.n]

    def to_fill(self, pe, s):
        if s >= self.n:
            pe.wait_ge(self.free[s % self.n], s // self.n)

    def filled(self, ins, s):
        ins.then_inc(self.full[s % self.n], 1)

    def to_read(self, eng, s):
        eng.wait_ge(self.full[s % self.n], s // self.n + 1)

    def emptied(self, ins, s):
        ins.then_inc(self.free[s % self.n], 1)

    def after_read(self, eng, s):
        eng.wait_ge(self.free[s % self.n], s // self.n + 1)


INPUTS = [
    "x", "positions", "norm_w", "w_in", "lam_re", "lam_im", "log_dt", "b_re", "b_im", "c_re", "c_im", "d_skip",
    "w_glu", "q_norm_w", "k_norm_w", "w_ssm_out", "w_attn_out", "w_o", "norm_mix_2", "w_in_2", "hg_lb_2",
    "hg_out_norm_2", "da_q_norm_2", "da_k_norm_2", "da_lambda_2", "da_out_norm_2", "w_branch_hg_2",
    "w_branch_da_2", "w_out_2", "norm_moe_2", "w_router_group_2", "b_router_group_2", "w_router_expert_2",
    "b_router_expert_2", "w1_2", "w3_2", "w2_2",
]

NSEM_RING = 8
UNIT = 4096
SLOTS_BLOCKS = 4
W1COLS = {"u": 0, "zs": 1024, "q": 2048, "k": 3584, "v": 5120, "za": 6656, "rs": 7168, "ra": 8192}
ATT_SCALE = 0.125
GROUPS = 3
HEADS = 8
HD = 64


def col_chunk(w, c0):
    return w[:, c0:c0 + 512].rearrange("(k p) n -> p k n", p=P)


def build(nc, A, out):
    stack = ExitStack()
    with stack:
        def sb(name, shape, dt=F32):
            return stack.enter_context(nc.sbuf_tensor(name, shape, dt))

        def sem(name):
            return stack.enter_context(nc.semaphore(name))

        mem = sb("mem", [P, 6 * UNIT + 18944])
        ring = mem[:, 0:NSEM_RING * UNIT].rearrange("p (s n) -> p s n", s=NSEM_RING)
        area = mem[:, 6 * UNIT:]
        xres = sb("xres", [P, TT, D])
        xn = sb("xn", [P, TT, D])
        hT = sb("hT", [P, KD, T])
        con = sb("con", [P, NCONST])
        small = sb("small", [P, 1024])
        psum = stack.enter_context(nc.psum_tensor("psum", [P, 8, 512], F32))
        banks = [psum[:, i, :] for i in range(8)]

        def C(name):
            a, w = CONST_AT[name]
            return con[:, a:a + w]

        ident = C("ident")
        halfpi, eps = C("halfpi"), C("eps")

        def carve(start, sizes):
            got, at = [], start
            for n in sizes:
                got.append(area[:, at:at + n])
                at += n
            assert at <= 18944, at
            return got

        def bc(ap, shape):
            return ap.to_broadcast(shape)

        units = []

        def add_unit(name, src, width=UNIT, k=KD):
            units.append((name, src, width, k))

        w_in = A["w_in"][0]
        for n in range(2):
            add_unit(f"u{n}", col_chunk(w_in, W1COLS["u"] + 512 * n))
        for key in "qkv":
            for n in range(3):
                add_unit(f"{key}{n}", col_chunk(w_in, W1COLS[key] + 512 * n))
        for n in range(2):
            add_unit(f"zs{n}", col_chunk(w_in, W1COLS["zs"] + 512 * n))
        for n in range(2):
            add_unit(f"rs{n}", col_chunk(w_in, W1COLS["rs"] + 512 * n))
        for n in range(2):
            add_unit(f"glu{n}", col_chunk(A["w_glu"][0], 512 * n))
        add_unit("za", col_chunk(w_in, W1COLS["za"]))
        for n in range(2):
            add_unit(f"so{n}", col_chunk(A["w_ssm_out"][0], 512 * n))
        for n in range(2):
            add_unit(f"ra{n}", col_chunk(w_in, W1COLS["ra"] + 512 * n))
        add_unit("ao", A["w_attn_out"][0].rearrange("(k p) n -> p k n", p=P), k=4)
        for n in range(2):
            add_unit(f"wo{n}", col_chunk(A["w_o"][0], 512 * n))
        n_units1 = len(units)
        w_in2 = A["w_in_2"][0]
        for key, c0 in (("hf", 512), ("hq", 0), ("dq", 2048), ("dk", 2560), ("hi", 1024), ("dv", 3072), ("hog", 1536),
                        ("ghg0", 3584), ("ghg1", 4096), ("gda0", 4608), ("gda1", 5120)):
            add_unit(key, col_chunk(w_in2, c0))
        for key in ("bhg", "bda"):
            add_unit(key, A["w_branch_hg_2" if key == "bhg" else "w_branch_da_2"][0].rearrange("(k p) n -> p k n", p=P), k=4)
        for n in range(2):
            add_unit(f"wout{n}", col_chunk(A["w_out_2"][0], 512 * n))
        n_blocks = len(units)
        order = {u[0]: i for i, u in enumerate(units)}

        slot_loaded = [sem(f"slot{s}_loaded") for s in range(NSEM_RING)]
        last_fill = {}

        def load_unit(sp, n):
            name, src, width, k = units[n]
            s = n % SLOTS_BLOCKS
            if n >= SLOTS_BLOCKS:
                pj.to_read(sp, last_fill[units[n - SLOTS_BLOCKS][0]])
            sp.dma_start(ring[:, s, :].rearrange("p (k n) -> p k n", k=k), src).then_inc(slot_loaded[s], 16)

        def unit_ready(pe, name):
            n = order[name]
            pe.wait_ge(slot_loaded[n % SLOTS_BLOCKS], 16 * (n // SLOTS_BLOCKS + 1))
            k = units[n][3]
            return ring[:, n % SLOTS_BLOCKS, :].rearrange("p (k n) -> p k n", k=k)

        def project(pe, w, i, dst, lhs, c0=0):
            nk = lhs.shape[1]
            for k in range(nk):
                ins = pe.matmul(dst, lhs[:, k, P * i:P * i + P], w[:, k, c0:c0 + 512], start=(k == 0), stop=(k == nk - 1))
            return ins

        def project_t(pe, w, m, dst, rhs):
            nk = rhs.shape[1]
            for k in range(nk):
                ins = pe.matmul(dst, w[:, k, P * m:P * m + P], rhs[:, k, :], start=(k == 0), stop=(k == nk - 1))
            return ins

        EXPERTS, GROUP_OF, SLOTS = 32, 4, 32
        N_GROUPS, UNITS = EXPERTS // GROUP_OF, 12
        FF = 512
        expert_rows = [A[name][0].rearrange("e (p k) n -> p e (k n)", p=P) for name in ("w1_2", "w3_2", "w2_2")]
        earlier_loads = [n_blocks // SLOTS_BLOCKS] * SLOTS_BLOCKS + [0] * (NSEM_RING - SLOTS_BLOCKS)
        assert n_blocks % SLOTS_BLOCKS == 0 and 2 * UNITS % NSEM_RING == 0

        def load_expert_unit(sp, m, group, half=0):
            src = expert_rows[m // 4][:, bass.ds(group * GROUP_OF, GROUP_OF), 1024 * (m % 4):1024 * (m % 4) + 1024]
            s = (half * UNITS + m) % NSEM_RING
            sp.dma_start(ring[:, s, :].rearrange("p (e n) -> p e n", e=GROUP_OF), src).then_inc(slot_loaded[s], 16)

        work = mem[:, SLOTS_BLOCKS * UNIT:6 * UNIT]
        phase = work[:, 0:1024].rearrange("p (b n) -> p b n", b=2)
        sin_t = work[:, 1024:2048].rearrange("p (b n) -> p b n", b=2)
        cos_t = work[:, 2048:3072].rearrange("p (b n) -> p b n", b=2)
        abs_t = work[:, 3072:3584]
        tmp_a, tmp_b = work[:, 3584:4096], work[:, 4096:4608]
        rot_re, rot_im = work[:, 4608:5120], work[:, 5120:5632]
        scan_re = work[:, 5632:6656].rearrange("p (b n) -> p b n", b=2)
        scan_im = work[:, 6656:7680].rearrange("p (b n) -> p b n", b=2)
        pool_tmp = work[:, 7680:8192]
        uT_, BTr_, BTi_, CTr_, CTi_, fa_, fb_, Hr_, Hi_, ptmp2, qT_, kT_, v_ = carve(
            0, [2048, 1024, 1024, 1024, 1024, 512, 512, 1024, 1024, 512, 3072, 3072, 3072])
        uT = uT_.rearrange("p (j t) -> p j t", j=8)
        BTr, BTi = (b.rearrange("p (j s) -> p j s", j=8) for b in (BTr_, BTi_))
        CTr, CTi = (b.rearrange("p (j s) -> p j s", j=8) for b in (CTr_, CTi_))
        fa, fb = (b.rearrange("p (t n) -> p t n", t=32) for b in (fa_, fb_))
        Hr, Hi = (b.rearrange("p (b n) -> p b n", b=2) for b in (Hr_, Hi_))
        qT, kT = (b.rearrange("p (g h t) -> p g h t", g=3, h=4) for b in (qT_, kT_))
        v_tok = v_.rearrange("p (i g n) -> p i g n", i=2, g=3)
        b_in = qT_[:, 0:1024].rearrange("p (c t n) -> p c t n", c=2, t=32)
        bblk_ = [qT_[:, 1024:2048], qT_[:, 2048:3072]]
        bblk = [b.rearrange("p (t w n) -> p t w n", t=32, w=2) for b in bblk_]
        c_in = kT_[:, 0:1024].rearrange("p (c j n) -> p c j n", c=2, j=8)
        cblk_ = [kT_[:, 1024:2048], kT_[:, 2048:3072]]
        cblk = [b.rearrange("p (j w n) -> p j w n", j=8, w=2) for b in cblk_]
        setup_tmp = v_[:, 0:512].rearrange("p (t n) -> p t n", t=32)
        rows = v_[0:32, 512:512 + 20 * 128].rearrange("p (a n) -> p a n", a=20)
        (LR, LI, DTB, LRDT, LIDT, FR, RN, MAG, SN, AB, CS, ABR, ABI, DEN, RDEN, NR, T1, T2, FRE, FIM) = range(20)
        stag = [xres[:, :, :].rearrange("p i n -> p (i n)")[:, 0:1024], xres[:, :, :].rearrange("p i n -> p (i n)")[:, 1024:2048],
                xn[:, :, :].rearrange("p i n -> p (i n)")[:, 0:1024]]
        sq_tmp = xn[:, 1, :]

        normw = small[:, 0:8]
        dskip = small[:, 8:16]
        ss = small[:, 16:18]
        rstd = small[:, 18:20]
        pst = small[:, 20:148].rearrange("p (a t) -> p a t", a=4)
        mag_c, ang_c, fre_c, fim_c = (pst[:, a, :] for a in range(4))
        qkw = small[:, 148:532].rearrange("p (c n) -> p c n", c=6)
        posi = sb("posi", [P, 2], I32)
        posf = small[:, 532:534]
        ropang = small[:, 534:550].rearrange("p (i n) -> p i n", i=2)
        roprn = small[:, 550:566].rearrange("p (i n) -> p i n", i=2)
        ropsin = small[:, 566:582].rearrange("p (i n) -> p i n", i=2)
        ropcos = small[:, 582:598].rearrange("p (i n) -> p i n", i=2)
        hss = small[:, 600:616]
        hrs = small[:, 616:632]
        ropt = small[:, 700:956].rearrange("p (n m) -> p n m", n=2)
        ldt = small[0:32, 632:634]
        dt2 = small[0:32, 634:636]
        mx = small[:, 640:642]
        sm = small[:, 642:644]
        rs = small[:, 644:646]

        pj = Banks([banks[0], banks[1]], [sem("pj0_full"), sem("pj1_full")], [sem("pj0_free"), sem("pj1_free")])
        tp = Banks([banks[2], banks[3]], [sem("tp0_full"), sem("tp1_full")], [sem("tp0_free"), sem("tp1_free")])
        PJ_U, PJ_QKV, PJ_ATT, PJ_RS, PJ_GLU, PJ_ZA, PJ_SO, PJ_RA, PJ_AO, PJ_WO, PJ_END1 = (
            0, 8, 26, 50, 54, 62, 64, 68, 72, 76, 80)
        TP_X, TP_PRM, TP_B, TP_C, TP_QK, TP_ATT, TP_O, TP_M, TP_END1 = 0, 4, 5, 9, 13, 25, 49, 51, 55

        def att_fill(a):
            return PJ_ATT + a + min((a + 1) // 2 + 1, 8)

        def zs_fill(m):
            return PJ_ATT + max(3 * m - 1, 0)

        for name, s in ([(f"u{n}", PJ_U + 4 * n + 3) for n in range(2)]
                        + [("qkv"[n // 3] + str(n % 3), PJ_QKV + 2 * n + 1) for n in range(9)]
                        + [(f"zs{n}", zs_fill(4 * n + 3)) for n in range(2)]
                        + [(f"glu{n}", PJ_GLU + 4 * n + 3) for n in range(2)]
                        + [(f"rs{n}", PJ_RS + 2 * n + 1) for n in range(2)]
                        + [(f"so{n}", PJ_SO + 2 * n + 1) for n in range(2)]
                        + [("za", PJ_ZA + 1)] + [(f"ra{n}", PJ_RA + 2 * n + 1) for n in range(2)]
                        + [("ao", PJ_AO + 3)] + [(f"wo{n}", PJ_WO + 2 * n + 1) for n in range(2)]):
            last_fill[name] = s

        con_in, x_in, par_in, bc_in, xre_in, normw_in = (sem(s) for s in ("con_in", "x_in", "par_in", "bc_in", "xre_in", "normw_in"))
        act1, dve1, pool1 = Signal(sem("act_step1")), Signal(sem("dve_step1")), Signal(sem("pool_step1"))
        sq_done, var_done, xn_ready = sem("sq_done"), sem("var_done"), Signal(sem("xn_ready"))
        dt_ready, decay_in, decay_ready = sem("dt_ready"), sem("decay_in"), sem("decay_ready")
        prm_ready, prm_copied = sem("prm_ready"), sem("prm_copied")
        blk_ready = Signal(sem("blk_ready"))
        phase_ready, trig_ready = Signal(sem("phase_ready")), Signal(sem("trig_ready"))
        bu_full, bu_free = sem("bu_full"), Signal(sem("bu_free"))
        scan_done, state_ready, y_part = Signal(sem("scan_done")), Signal(sem("state_ready")), sem("y_part")
        y_free = Signal(sem("y_free"))
        sq_ready = sem("sq_ready")
        rope_in, rope_ready = sem("rope_in"), sem("rope_ready")
        hss_ready, hrs_ready, qk_ready = sem("hss_ready"), sem("hrs_ready"), Signal(sem("qk_ready"))
        y_all = sem("y_all")

        lb2 = small[:, 8:16].rearrange("p (r h) -> p r h", r=2)
        hgain = small[:, 28:156]
        dgain = small[:, 156:284].rearrange("p (c n) -> p c n", c=2)
        ogain = small[:, 284:412]
        lamv = small[:, 412:668].rearrange("p (r n) -> p r n", r=4)
        par2_in = sem("par2_in")
        mixw = small[:, 956:964]
        ssq2, ss2, rstd2 = small[:, 964:968].rearrange("p (c i) -> p c i", c=2), small[:, 968:970], small[:, 970:972]
        mixw_in, sq2_done, ss2_ready, root2_ready = (sem(s) for s in ("mixw_in", "sq2_done", "ss2_ready", "root2_ready"))
        xT2_full, diag2_ready, rows2_full, rows2_ready, hT2_ready = (sem(s) for s in (
            "xT2_full", "diag2_ready", "rows2_full", "rows2_ready", "hT2_ready"))
        diag2, rows2, square2 = work[:, 0:256], work[:, 256:512], work[:, 512:2560]

        PAIRS = 16
        s_sb = [work[:, 768 * n:768 * n + 768] for n in range(2)]
        p_sb = [work[:, 1536 + 768 * n:2304 + 768 * n] for n in range(2)]
        pT = [work[:, 3072 + 768 * n:3840 + 768 * n] for n in range(2)]
        o_tok = work[:, 4608:5632].rearrange("p (i n) -> p i n", i=2)
        gate_a = work[:, 5632:6656].rearrange("p (i n) -> p i n", i=2)
        gate_b = work[:, 6656:7680].rearrange("p (i n) -> p i n", i=2)
        gs_, m_, oaT_, mT_ = carve(2048, [2048, 2048, 1024, 2048])
        ths_, tha_ = carve(11776, [2048, 2048])
        zs2_ = mT_
        gs, mT, zs2 = (b.rearrange("p (j t) -> p j t", j=8) for b in (gs_, mT_, zs2_))
        oaT = oaT_.rearrange("p (j t) -> p j t", j=4)
        m_tok, th_s, th_a = (b.rearrange("p (i n) -> p i n", i=2) for b in (m_, ths_, tha_))
        zt = [work[:, 6656 + 256 * n:6912 + 256 * n] for n in range(2)]
        gel = [gs_[:, 0:1024], m_[:, 0:1024], m_[:, 1024:2048]]
        rsum = small[:, 700:716]
        rrec = small[:, 716:732]
        nmax = small[:, 732:748]
        s_full, s_free, m_ready, p_ready = sem("s_full"), Signal(sem("s_free")), Signal(sem("m_ready")), sem("p_ready")
        gel_in, gel_th, g_ready = sem("gel_in"), sem("gel_th"), sem("g_ready")
        zt_ready, glu_used = sem("zt_ready"), sem("glu_used")
        th_za, oa_ready, m_done, x1_done = sem("th_za"), sem("oa_ready"), sem("m_done"), Signal(sem("x1_done"))
        th_s_ready, th_a_ready = sem("th_s_ready"), sem("th_a_ready")

        def heads_blocks():
            return [(2 * h + b, h, b, P * (b + 1)) for h in range(HEADS) for b in range(2)]

        def att_fills(a):
            first = TP_ATT + 3 * (a // 2) + (a % 2)
            return range(first, first + 1 + a % 2)
        scope = ExitStack()
        block = scope.enter_context(nc.Block())

        @block.sync
        def _(sp):
            sp.dma_start(xres[:, :, :], A["x"][0].rearrange("(i p) n -> p i n", p=P)).then_inc(x_in, 16)
            sp.dma_start(con[:, :], A["constants"]).then_inc(con_in, 16)
            sp.dma_start(normw, A["norm_w"][0].rearrange("(k p) -> p k", p=P), allow_slow_non_contiguous=True).then_inc(normw_in, 16)
            load_unit(sp, 0)
            sp.wait_ge(par_in, 16 * 7)
            sp.wait_ge(bc_in, 16 * 4)
            for n in range(1, n_units1 - 8):
                load_unit(sp, n)
            sp.wait_ge(qk_ready.sem, 6)
            for s in range(2):
                tp.after_read(sp, TP_QK + 10 + s)
            sp.dma_start(xres[:, :, :], A["x"][0].rearrange("(i p) n -> p i n", p=P)).then_inc(xre_in, 16)
            for n in range(n_units1 - 8, n_units1 + SLOTS_BLOCKS):
                load_unit(sp, n)

        @block.gpsimd
        def _(pool):
            def col8(dst, src):
                pool.dma_start(dst, src.rearrange("(k p) -> p k", p=P), allow_slow_non_contiguous=True).then_inc(par_in, 16)

            pool.dma_start(ldt, A["log_dt"][0].rearrange("(t w) -> t w", w=2)).then_inc(par_in, 16)
            pool.dma_start(rows[:, LR, :], A["lam_re"][0].rearrange("(t w) n -> t (w n)", w=2)).then_inc(par_in, 16)
            pool.dma_start(rows[:, LI, :], A["lam_im"][0].rearrange("(t w) n -> t (w n)", w=2)).then_inc(par_in, 16)
            col8(dskip, A["d_skip"][0])
            for c, name in enumerate(("q_norm_w", "k_norm_w")):
                pool.dma_start(qkw[:, 3 * c:3 * c + 3, :], A[name][0].partition_broadcast(P)).then_inc(par_in, 16)
            pool.dma_start(posi[:, :], A["positions"][0].rearrange("(i p) -> p i", p=P), allow_slow_non_contiguous=True).then_inc(par_in, 16)
            pool.dma_start(mixw, A["norm_mix_2"][0].rearrange("(k p) -> p k", p=P), allow_slow_non_contiguous=True).then_inc(mixw_in, 16)
            for c, name in enumerate(("b_re", "b_im")):
                pool.dma_start(b_in[:, c], A[name][0].rearrange("(t w) n p -> (w n) t p", w=2)).then_inc(bc_in, 16)
            for c, name in enumerate(("c_re", "c_im")):
                pool.dma_start(c_in[:, c], A[name][0].rearrange("(j g) q n -> (g q) j n", j=8)).then_inc(bc_in, 16)

            for pr in range(PAIRS):
                b = pr % 2
                pool.wait_ge(scan_done.sem, pr + 1)
                if pr >= 2:
                    pool.wait_ge(y_part, pr - 1)
                link(pool, pool.tensor_tensor(Hr[:, b], cos_t[:, b], scan_re[:, b], ALU.mult), pool1)
                link(pool, pool.tensor_tensor(pool_tmp, sin_t[:, b], scan_im[:, b], ALU.mult), pool1)
                link(pool, pool.tensor_tensor(Hr[:, b], Hr[:, b], pool_tmp, ALU.subtract), pool1)
                link(pool, pool.tensor_tensor(Hi[:, b], cos_t[:, b], scan_im[:, b], ALU.mult), pool1)
                link(pool, pool.tensor_tensor(ptmp2, sin_t[:, b], scan_re[:, b], ALU.mult), pool1)
                link(pool, pool.tensor_tensor(Hi[:, b], Hi[:, b], ptmp2, ALU.add), state_ready)
            pool.wait_ge(y_free.sem, 8)
            pool.wait_ge(qk_ready.sem, 6)

            def load(dst, src, **kw):
                pool.dma_start(dst, src, **kw).then_inc(par2_in, 16)

            for r in range(2):
                load(lb2[:, r], A["hg_lb_2"][r].rearrange("(k p) -> p k", p=P), allow_slow_non_contiguous=True)
            load(hgain, A["hg_out_norm_2"][0].partition_broadcast(P))
            load(dgain[:, 0], A["da_q_norm_2"][0].partition_broadcast(P))
            load(dgain[:, 1], A["da_k_norm_2"][0].partition_broadcast(P))
            load(ogain, A["da_out_norm_2"][0].partition_broadcast(P))
            load(lamv, A["da_lambda_2"][0].partition_broadcast(P))

        @block.scalar
        def _(act):
            act.wait_ge(x_in, 16)
            act.activation(xn[:, 0, :], xres[:, 0, :], ACT.Square, accum_out=ss[:, 0:1])
            act.activation(xn[:, 1, :], xres[:, 1, :], ACT.Square, accum_out=ss[:, 1:2]).then_inc(sq_done, 1)
            act.wait_ge(sq_done, 1)
            act.wait_ge(con_in, 16)
            act.activation(rstd, ss, ACT.Sqrt, scale=1.0 / D, bias=eps).then_inc(var_done, 1)
            act.wait_ge(normw_in, 16)
            for s in range(4):
                tp.to_read(act, TP_X + s)
                for h in range(2):
                    k = 2 * s + h
                    ins = act.activation(hT[:, k, :], tp.tile(s)[:, 256 * h:256 * h + 256], ACT.Copy, scale=normw[:, k:k + 1])
                tp.emptied(ins, TP_X + s)
            act.wait_ge(par_in, 16 * 7)
            act.activation(dt2, ldt, ACT.Exp).then_inc(dt_ready, 1)
            act.wait_ge(decay_in, 1)
            act.activation(rows[:, MAG, :], rows[:, LRDT, :], ACT.Exp)
            act.activation(rows[:, SN, :], rows[:, FR, :], ACT.Sin, scale=TURN)
            link(act, act.activation(rows[:, AB, :], rows[:, FR, :], ACT.Abs), act1)
            act.activation(rows[:, CS, :], rows[:, AB, :], ACT.Sin, scale=-TURN, bias=halfpi[0:32, :]).then_inc(decay_ready, 1)
            act.wait_ge(rope_in, 1)
            act.activation(ropsin, ropang, ACT.Sin)
            link(act, act.activation(roprn, ropang, ACT.Abs), act1)
            act.activation(ropcos, roprn, ACT.Sin, scale=-1.0, bias=halfpi).then_inc(rope_ready, 1)
            for j in range(8):
                pj.to_read(act, PJ_U + j)
                pj.emptied(act.activation(uT[:, j, :], pj.tile(j)[:, 0:256], ACT.Copy), PJ_U + j)
            for n, (dst, sgn) in enumerate(((BTr_, 1.0), (BTi_, 1.0), (CTr_, 1.0), (CTi_, -1.0))):
                for h in range(2):
                    s = TP_B + 2 * n + h
                    tp.to_read(act, s)
                    tp.emptied(act.activation(dst[:, 512 * h:512 * h + 512], tp.tile(s)[:, :], ACT.Copy, scale=sgn), s)

            def trig(pr):
                b = pr % 2
                act.wait_ge(phase_ready.sem, pr + 1)
                if pr >= 2:
                    act.wait_ge(state_ready.sem, pr - 1)
                act.activation(sin_t[:, b], phase[:, b], ACT.Sin, scale=TURN)
                link(act, act.activation(abs_t, phase[:, b], ACT.Abs), act1)
                link(act, act.activation(cos_t[:, b], abs_t, ACT.Sin, scale=-TURN, bias=halfpi), trig_ready)

            trig(0)
            for h in range(18):
                if h >= 3 and h % 2 == 1 and (h - 3) // 2 < 6:
                    act.wait_ge(hss_ready, (h - 3) // 2 + 1)
                    act.activation(hrs, hss, ACT.Sqrt, scale=1.0 / HD, bias=eps).then_inc(hrs_ready, 1)
                if h + 1 < PAIRS:
                    trig(h + 1)
                if h >= 2 and h % 2 == 0 and (h - 2) // 2 < 6:
                    w = (h - 2) // 2
                    for i in range(2):
                        pj.after_read(act, PJ_QKV + 2 * w + i)
                    if w >= 1:
                        act.wait_ge(qk_ready.sem, w)
                    act.activation(sq_tmp, stag[w % 3], ACT.Square).then_inc(sq_ready, 1)
                u, i = h // 2, h % 2
                s = PJ_QKV + h
                pj.to_read(act, s)
                if u < 6:
                    if u >= 3:
                        for q in range(2):
                            tp.to_read(act, TP_QK + 2 * (u - 3) + q)
                    dst = stag[u % 3][:, 512 * i:512 * i + 512]
                else:
                    dst = v_tok[:, i, u - 6, :]
                pj.emptied(act.activation(dst, pj.tile(s)[:, :], ACT.Copy), s)
                if h >= 5 and h % 2 == 1 and (h - 5) // 2 < 6:
                    w = (h - 5) // 2
                    dst = (qT, kT)[w // 3][:, w % 3]
                    for q in range(2):
                        s = TP_QK + 2 * w + q
                        tp.to_read(act, s)
                        tp.emptied(act.activation(dst[:, 2 * q:2 * q + 2, :].rearrange("p h t -> p (h t)"), tp.tile(s)[:, :], ACT.Copy), s)
            for a, h, q, nk in heads_blocks():
                act.wait_ge(m_ready.sem, a + 1)
                if a >= 2:
                    for s in att_fills(a - 2):
                        tp.to_read(act, s)
                act.activation(p_sb[a % 2][:, 0:3 * nk], s_sb[a % 2][:, 0:3 * nk], ACT.Exp, bias=nmax[:, a:a + 1],
                               accum_out=rsum[:, a:a + 1]).then_inc(p_ready, 1)
                if a % 2 == 0:
                    m = a // 2
                    pj.to_read(act, zs_fill(m))
                    if m >= 2:
                        pj.after_read(act, zs_fill(m - 2))
                    act.activation(zt[m % 2], pj.tile(zs_fill(m))[:, 0:256], ACT.Tanh, scale=0.5).then_inc(zt_ready, 1)
                if a >= 2:
                    pj.to_read(act, att_fill(a - 2))
                for n, s in enumerate(att_fills(a)):
                    tp.to_read(act, s)
                    tp.emptied(act.activation(pT[a % 2][:, 384 * n:384 * n + 384], tp.tile(s)[:, 0:384], ACT.Copy), s)
            for n in range(2):
                act.wait_ge(gel_in, n + 1)
                act.activation(gel[1 + n], gel[1 + n], ACT.Tanh, scale=math.sqrt(2 / math.pi)).then_inc(gel_th, 1)
            for n in range(4):
                s = PJ_RS + n
                pj.to_read(act, s)
                pj.emptied(act.activation(th_s[:, n % 2, 512 * (n // 2):512 * (n // 2) + 512], pj.tile(s)[:, :], ACT.Tanh, scale=0.5), s)
            for m in range(8):
                s = PJ_GLU + m
                pj.to_read(act, s)
                if m >= 2:
                    act.wait_ge(glu_used, m - 1)
                else:
                    pj.after_read(act, zs_fill(6 + m))
                pj.emptied(act.activation(zt[m % 2], pj.tile(s)[:, 0:256], ACT.Tanh, scale=0.25), s)
            for n in range(2):
                s = PJ_ZA + n
                pj.to_read(act, s)
                act.activation(gate_a[:, n, :], pj.tile(s)[:, :], ACT.Tanh, scale=0.5).then_inc(th_za, 1)
            for n in range(4):
                s = PJ_RA + n
                pj.to_read(act, s)
                pj.emptied(act.activation(th_a[:, n % 2, 512 * (n // 2):512 * (n // 2) + 512], pj.tile(s)[:, :], ACT.Tanh, scale=0.5), s)
            for s in range(TP_O, TP_O + 2):
                tp.to_read(act, s)
                n = s - TP_O
                tp.emptied(act.activation(oaT_[:, 512 * n:512 * n + 512], tp.tile(s)[:, :], ACT.Copy), s)
            act.wait_ge(glu_used, 8)
            for s in range(TP_M, TP_M + 4):
                tp.to_read(act, s)
                n = s - TP_M
                tp.emptied(act.activation(mT_[:, 512 * n:512 * n + 512], tp.tile(s)[:, :], ACT.Copy, scale=1.0 / 16), s)
            act.activation(rstd2, eps.to_broadcast([P, 2]), ACT.Sqrt)
            for n in range(4):
                i, c = n % 2, n // 2
                pj.after_read(act, PJ_WO + n)
                ins = act.activation(square2[:, 512 * n:512 * n + 512], xres[:, i, 512 * c:512 * c + 512], ACT.Square, accum_out=ssq2[:, c, i:i + 1])
                ins.then_inc(sq2_done, 1)
            act.wait_ge(ss2_ready, 1)
            act.activation(rstd2, ss2, ACT.Sqrt, scale=1.0 / D, bias=eps).then_inc(root2_ready, 1)
            act.wait_ge(rows2_full, 1)
            act.activation(rows2, banks[2][:, 0:256], ACT.Copy).then_inc(rows2_ready, 1)

        @block.tensor
        def _(pe):
            pe.wait_ge(con_in, 16)
            pe.wait_ge(xn_ready.sem, 2)
            for s in range(4):
                tp.to_fill(pe, TP_X + s)
                for h in range(2):
                    k = 2 * s + h
                    for i in range(2):
                        ins = pe.transpose(tp.tile(s)[:, 256 * h + P * i:256 * h + P * i + P], xn[:, i, P * k:P * k + P], ident)
                tp.filled(ins, TP_X + s)
            for s in range(2):
                tp.after_read(pe, TP_X + 2 + s)
            for n in range(2):
                w = unit_ready(pe, f"u{n}")
                for m in range(4):
                    s = PJ_U + 4 * n + m
                    pj.to_fill(pe, s)
                    pj.filled(project_t(pe, w, m, pj.tile(s)[:, 0:256], hT), s)
            pe.wait_ge(prm_ready, 1)
            tp.to_fill(pe, TP_PRM)
            for a, r in enumerate((MAG, FR, FRE, FIM)):
                ins = pe.transpose(tp.tile(TP_PRM)[:, 32 * a:32 * a + 32], rows[:, r, :], ident[0:32, 0:32])
            tp.filled(ins, TP_PRM)
            for n, blk in enumerate((bblk_[0], bblk_[1], cblk_[0], cblk_[1])):
                pe.wait_ge(blk_ready.sem, min(n + 1, 2))
                for h in range(2):
                    s = TP_B + 2 * n + h
                    tp.to_fill(pe, s)
                    for q in range(4):
                        j = 4 * h + q
                        ins = pe.transpose(tp.tile(s)[:, P * q:P * q + P], blk[:, P * j:P * j + P], ident)
                    tp.filled(ins, s)

            def inputs_of_pair(pr):
                if pr >= 1:
                    pe.wait_ge(bu_free.sem, pr)
                j = pr // 2
                for w in range(2):
                    q = 2 * (pr % 2) + w
                    r = slice(32 * q, 32 * q + 32)
                    for n, BT in enumerate((BTr, BTi)):
                        ins = pe.matmul(banks[4 + w][:, 256 * n:256 * n + 256], BT[r, j, :], uT[r, j, :], start=True, stop=True)
                ins.then_inc(bu_full, 1)

            def outputs_of_pair(pr):
                pe.wait_ge(state_ready.sem, pr + 1)
                j = pr // 2
                if pr % 2 == 0 and j >= 2:
                    pe.wait_ge(y_free.sem, j - 1)
                for w in range(2):
                    q = 2 * (pr % 2) + w
                    dst = banks[6 + j % 2][32 * q:32 * q + 32, 0:256]
                    b, c = pr % 2, slice(256 * w, 256 * w + 256)
                    pe.matmul(dst, CTr[:, j, 32 * q:32 * q + 32], Hr[:, b, c], start=True, stop=False, tile_position=(0, 32 * q))
                    ins = pe.matmul(dst, CTi[:, j, 32 * q:32 * q + 32], Hi[:, b, c], start=False, stop=True, tile_position=(0, 32 * q))
                ins.then_inc(y_part, 1)

            for s in range(2):
                tp.after_read(pe, TP_C + 2 + s)
            for s in range(2):
                pj.after_read(pe, PJ_U + 6 + s)
            for h in range(18):
                u, i = h // 2, h % 2
                name = "qkv"[u // 3] + str(u % 3)
                if h < PAIRS:
                    inputs_of_pair(h)
                w = unit_ready(pe, name)
                s = PJ_QKV + h
                pj.to_fill(pe, s)
                pj.filled(project(pe, w, i, pj.tile(s)[:, :], hT), s)
                if h >= 2:
                    outputs_of_pair(h - 2)
                if h >= 5 and h % 2 == 1 and (h - 5) // 2 < 6:
                    w = (h - 5) // 2
                    pe.wait_ge(qk_ready.sem, w + 1)
                    for q in range(2):
                        s = TP_QK + 2 * w + q
                        tp.to_fill(pe, s)
                        for hp in range(2):
                            for i2 in range(2):
                                ins = pe.transpose(tp.tile(s)[:, 256 * hp + P * i2:256 * hp + P * i2 + P],
                                                   stag[w % 3][:, 512 * i2 + P * (2 * q + hp):512 * i2 + P * (2 * q + hp) + P], ident)
                        tp.filled(ins, s)

            def scores(a, h, q, nk):
                if a == 0:
                    pe.wait_ge(bu_free.sem, PAIRS)
                elif a == 1:
                    pe.wait_ge(y_free.sem, 8)
                else:
                    pe.wait_ge(s_free.sem, a - 1)
                r = slice(64 * (h % 2), 64 * (h % 2) + 64)
                for g in range(3):
                    at = g * nk
                    ins = pe.matmul(banks[4 + 2 * (a % 2) + at // 512][:, at % 512:at % 512 + nk],
                                    qT[r, g, h // 2, P * q:P * q + P], kT[r, g, h // 2, 0:nk], start=True, stop=True)
                ins.then_inc(s_full, 1)

            def turn_p(a, q):
                pe.wait_ge(p_ready, a + 1)
                for n, s in enumerate(att_fills(a)):
                    tp.to_fill(pe, s)
                    for c in range(3):
                        at = P * (3 * n + c)
                        ins = pe.transpose(tp.tile(s)[:, P * c:P * c + P], p_sb[a % 2][:, at:at + P], ident)
                    tp.filled(ins, s)

            def weigh_values(a, h, q):
                for s in att_fills(a):
                    tp.after_read(pe, s)
                s = att_fill(a)
                pj.to_fill(pe, s)
                nb = q + 1
                for c in range(3 * nb):
                    ins = pe.matmul(pj.tile(s)[:, 0:64], pT[a % 2][:, P * c:P * c + P],
                                    v_tok[:, c % nb, c // nb, 64 * h:64 * h + 64], start=(c == 0), stop=(c == 3 * nb - 1))
                pj.filled(ins, s)

            for s in range(2):
                pj.after_read(pe, PJ_QKV + 16 + s)
                tp.after_read(pe, TP_QK + 10 + s)
            pieces = heads_blocks()
            scores(*pieces[0])
            for a, h, q, nk in pieces:
                if a + 1 < len(pieces):
                    scores(*pieces[a + 1])
                if a % 2 == 0:
                    m = a // 2
                    w = unit_ready(pe, f"zs{m // 4}")
                    pj.to_fill(pe, zs_fill(m))
                    pj.filled(project_t(pe, w, m % 4, pj.tile(zs_fill(m))[:, 0:256], hT), zs_fill(m))
                turn_p(a, q)
                if a >= 1:
                    weigh_values(a - 1, pieces[a - 1][1], pieces[a - 1][2])
            weigh_values(15, 7, 1)

            def project_all(names, first, lhs):
                for n, name in enumerate(names):
                    w = unit_ready(pe, name)
                    for i in range(2):
                        s = first + 2 * n + i
                        pj.to_fill(pe, s)
                        pj.filled(project(pe, w, i, pj.tile(s)[:, :], lhs), s)

            project_all(["rs0", "rs1"], PJ_RS, hT)
            pe.wait_ge(g_ready, 2)
            for m in range(8):
                w = unit_ready(pe, f"glu{m // 4}")
                pj.to_fill(pe, PJ_GLU + m)
                pj.filled(project_t(pe, w, m % 4, pj.tile(PJ_GLU + m)[:, 0:256], uT), PJ_GLU + m)

            project_all(["za"], PJ_ZA, hT)
            pe.wait_ge(glu_used, 8)
            project_all(["so0", "so1"], PJ_SO, gs)
            project_all(["ra0", "ra1"], PJ_RA, hT)
            pe.wait_ge(oa_ready, 2)
            for s in range(TP_O, TP_O + 2):
                tp.to_fill(pe, s)
                for n in range(4):
                    k, i = 2 * (s - TP_O) + n // 2, n % 2
                    ins = pe.transpose(tp.tile(s)[:, P * n:P * n + P], o_tok[:, i, P * k:P * k + P], ident)
                tp.filled(ins, s)
            for s in range(TP_O, TP_O + 2):
                tp.after_read(pe, s)
            w = unit_ready(pe, "ao")
            for n in range(4):
                s = PJ_AO + n
                pj.to_fill(pe, s)
                pj.filled(project(pe, w, n % 2, pj.tile(s)[:, :], oaT, c0=512 * (n // 2)), s)
            pe.wait_ge(m_done, 4)
            for s in range(TP_M, TP_M + 4):
                tp.to_fill(pe, s)
                for n in range(4):
                    k, i = 2 * (s - TP_M) + n // 2, n % 2
                    ins = pe.transpose(tp.tile(s)[:, P * n:P * n + P], m_tok[:, i, P * k:P * k + P], ident)
                tp.filled(ins, s)
            for s in range(TP_M + 2, TP_M + 4):
                tp.after_read(pe, s)


            def turn_x(chunks, i, ins=None):
                for k in chunks:
                    ins = pe.transpose(banks[4 + k // 2][:, 256 * (k % 2) + P * i:256 * (k % 2) + P * i + P],
                                       xres[:, i, P * k:P * k + P], ident)
                return ins

            for n in range(4):
                w = unit_ready(pe, f"wo{n // 2}")
                s = PJ_WO + n
                pj.to_fill(pe, s)
                pj.filled(project(pe, w, n % 2, pj.tile(s)[:, :], mT), s)
                if n == 2:
                    pe.wait_ge(s_free.sem, 16)
                    for i in range(2):
                        pj.after_read(pe, PJ_WO + i)
                        turn_x(range(4), i)
            for i in range(2):
                pj.after_read(pe, PJ_WO + 2 + i)
                ins = turn_x(range(4, 8), i)
            ins.then_inc(xT2_full, 1)
            pe.wait_ge(diag2_ready, 1)
            for s in range(TP_M + 2, TP_M + 4):
                tp.after_read(pe, s)
            pe.matmul(banks[2][:, 0:256], C("ones"), diag2, start=True, stop=True).then_inc(rows2_full, 1)

        @block.vector
        def _(dve):
            dve.wait_ge(var_done, 1)
            link(dve, dve.reciprocal(rstd, rstd), dve1)
            for i in range(2):
                link(dve, dve.tensor_scalar(xn[:, i, :], xres[:, i, :], rstd[:, i:i + 1], None, ALU.mult), xn_ready)
            dve.wait_ge(dt_ready, 1)
            R = lambda a: rows[:, a, :]
            R2 = lambda a: rows[:, a, :].rearrange("p (w n) -> p w n", w=2)
            link(dve, dve.tensor_copy(R2(DTB), bc(dt2.unsqueeze(2), [32, 2, 64])), dve1)
            link(dve, dve.tensor_tensor(R(LRDT), R(LR), R(DTB), ALU.mult), dve1)
            link(dve, dve.tensor_tensor(R(LIDT), R(LI), R(DTB), ALU.mult), dve1)
            link(dve, dve.tensor_scalar(R(LIDT), R(LIDT), 1.0 / (2 * math.pi), None, ALU.mult), dve1)
            link(dve, dve.tensor_scalar(R(RN), R(LIDT), ROUND, ROUND, ALU.add, ALU.subtract), dve1)
            link(dve, dve.tensor_tensor(R(FR), R(LIDT), R(RN), ALU.subtract), dve1)
            dve.tensor_copy(posf, posi[:, :]).then_inc(decay_in, 1)
            dve.wait_ge(decay_in, 1)
            dve.wait_ge(con_in, 16)
            for i in range(2):
                link(dve, dve.tensor_scalar(ropang[:, i, :], C("inv_freq"), posf[:, i:i + 1], None, ALU.mult), dve1)
            link(dve, dve.tensor_scalar(roprn, ropang, 1.0 / (2 * math.pi), None, ALU.mult), dve1)
            link(dve, dve.tensor_scalar(roprn, roprn, ROUND, ROUND, ALU.add, ALU.subtract), dve1)
            c1 = 6.28125
            c2 = float(np.float32(np.round((2 * math.pi - c1) * 2 ** 20) / 2 ** 20))
            c3 = 2 * math.pi - c1 - c2
            for c in (c1, c2, c3):
                link(dve, dve.scalar_tensor_tensor(out=ropang, in0=roprn, scalar=-c, in1=ropang, op0=ALU.mult, op1=ALU.add), dve1)
            dve.tensor_scalar(ropang, ropang, 3.1415925, -3.1415925, ALU.min, ALU.max).then_inc(rope_in, 1)
            dve.wait_ge(decay_ready, 1)
            link(dve, dve.tensor_tensor(R(ABR), R(MAG), R(CS), ALU.mult), dve1)
            link(dve, dve.tensor_tensor(R(ABI), R(MAG), R(SN), ALU.mult), dve1)
            link(dve, dve.tensor_tensor(R(DEN), R(LR), R(LR), ALU.mult), dve1)
            link(dve, dve.tensor_tensor(R(T1), R(LI), R(LI), ALU.mult), dve1)
            link(dve, dve.tensor_tensor(R(DEN), R(DEN), R(T1), ALU.add), dve1)
            link(dve, dve.reciprocal(R(RDEN), R(DEN)), dve1)
            link(dve, dve.tensor_scalar(R(NR), R(ABR), 1.0, None, ALU.subtract), dve1)
            link(dve, dve.tensor_tensor(R(T1), R(NR), R(LR), ALU.mult), dve1)
            link(dve, dve.tensor_tensor(R(T2), R(ABI), R(LI), ALU.mult), dve1)
            link(dve, dve.tensor_tensor(R(T1), R(T1), R(T2), ALU.add), dve1)
            link(dve, dve.tensor_tensor(R(FRE), R(T1), R(RDEN), ALU.mult), dve1)
            link(dve, dve.tensor_tensor(R(T1), R(ABI), R(LR), ALU.mult), dve1)
            link(dve, dve.tensor_tensor(R(T2), R(NR), R(LI), ALU.mult), dve1)
            link(dve, dve.tensor_tensor(R(T1), R(T1), R(T2), ALU.subtract), dve1)
            dve.tensor_tensor(R(FIM), R(T1), R(RDEN), ALU.mult).then_inc(prm_ready, 1)
            dve.wait_ge(prm_ready, 1)
            dve.wait_ge(bc_in, 64)
            par = C("parity")
            for n in range(2):
                for w in range(2):
                    ins = dve.tensor_scalar(cblk[n][:, :, w, :], c_in[:, n], par[:, w:w + 1], None, ALU.mult)
                    link(dve, ins, dve1)
            for n in range(2):
                link(dve, dve.memset(bblk_[n], 0.0), dve1)
            tp.to_read(dve, TP_PRM)
            tp.emptied(dve.tensor_copy(pst.rearrange("p a t -> p (a t)"), tp.tile(TP_PRM)[:, 0:128]), TP_PRM)
            tp.after_read(dve, TP_PRM)
            fre3, fim3 = (bc(a.unsqueeze(2), [P, 32, 16]) for a in (fre_c, fim_c))
            b_out = fb_.rearrange("p (t n) -> p t n", t=32)
            for n, (x0, x1, op) in enumerate(((b_in[:, 0], b_in[:, 1], ALU.subtract), (b_in[:, 1], b_in[:, 0], ALU.add))):
                link(dve, dve.tensor_tensor(setup_tmp, x1, fim3, ALU.mult), dve1)
                link(dve, dve.tensor_tensor(b_out, x0, fre3, ALU.mult), dve1)
                for w in range(2):
                    r = slice(64 * w, 64 * w + 64)
                    ins = dve.tensor_tensor(bblk[n][r, :, w, :], b_out[r], setup_tmp[r], op)
                    if w == 0:
                        link(dve, ins, dve1)
                    else:
                        link(dve, ins, blk_ready)
            it = bc(C("iota")[:, 0:16].unsqueeze(1), [P, 32, 16])
            ang16 = rs_ang = setup_tmp[:, 0:2, :].rearrange("p t n -> p (t n)")
            link(dve, dve.tensor_tensor(fb, bc(ang_c.unsqueeze(2), [P, 32, 16]), it, ALU.mult), dve1)
            link(dve, dve.tensor_scalar(fa, fb, ROUND, ROUND, ALU.add, ALU.subtract), dve1)
            link(dve, dve.tensor_tensor(fb, fb, fa, ALU.subtract), dve1)
            link(dve, dve.tensor_scalar(ang16, ang_c, 16.0, None, ALU.mult), dve1)
            link(dve, dve.tensor_scalar(fa_[:, 0:32], ang16, ROUND, ROUND, ALU.add, ALU.subtract), dve1)
            link(dve, dve.tensor_tensor(ang16, ang16, fa_[:, 0:32], ALU.subtract), dve1)
            link(dve, dve.tensor_copy(ang_c, ang16), dve1)
            link(dve, dve.tensor_tensor(fa, bc(ang_c.unsqueeze(2), [P, 32, 16]), it, ALU.mult), dve1)
            link(dve, dve.tensor_scalar(setup_tmp, fa, ROUND, ROUND, ALU.add, ALU.subtract), dve1)
            link(dve, dve.tensor_tensor(fa, fa, setup_tmp, ALU.subtract), dve1)

            def after(n):
                dve.wait_ge(dve1.sem, n)

            def angle_sums(pr):
                b = pr % 2
                if pr >= 2:
                    dve.wait_ge(trig_ready.sem, pr - 1)
                ph = phase[:, b].rearrange("p (w a b) -> p w a b", w=2, a=16)
                for w in range(2):
                    done = mark(dve.tensor_tensor(ph[:, w], bc(fa[:, 2 * pr + w, :].unsqueeze(2), [P, 16, 16]),
                                                  bc(fb[:, 2 * pr + w, :].unsqueeze(1), [P, 16, 16]), ALU.add), dve1)
                return done

            def whole_turns(pr):
                return mark(dve.tensor_scalar(rot_im, phase[:, pr % 2], ROUND, ROUND, ALU.add, ALU.subtract), dve1)

            def take_turns_off(pr):
                mark(dve.tensor_tensor(phase[:, pr % 2], phase[:, pr % 2], rot_im, ALU.subtract), phase_ready)

            def rotate_and_scan(pr):
                b = pr % 2
                more = pr + 1 < PAIRS
                if more:
                    summed = angle_sums(pr + 1)
                dve.wait_ge(bu_full, pr + 1)
                dve.wait_ge(trig_ready.sem, pr + 1)
                bur, bui = psum[:, 4:6, 0:256], psum[:, 4:6, 256:512]
                two = lambda ap: ap.rearrange("p (w n) -> p w n", w=2)
                mark(dve.tensor_tensor(two(tmp_a), two(cos_t[:, b]), bur, ALU.mult), dve1)
                products = mark(dve.tensor_tensor(two(tmp_b), two(sin_t[:, b]), bui, ALU.mult), dve1)
                if more:
                    after(summed)
                    turns = whole_turns(pr + 1)
                after(products)
                rotated = mark(dve.tensor_tensor(rot_re, tmp_a, tmp_b, ALU.add), dve1)
                if more:
                    after(turns)
                    take_turns_off(pr + 1)
                after(rotated)
                mark(dve.tensor_tensor(two(tmp_a), two(cos_t[:, b]), bui, ALU.mult), dve1)
                link(dve, dve.tensor_tensor(two(tmp_b), two(sin_t[:, b]), bur, ALU.mult), bu_free)
                if more:
                    dve.wait_ge(phase_ready.sem, pr + 2)
                rotated = mark(dve.tensor_tensor(rot_im, tmp_a, tmp_b, ALU.subtract), dve1)
                if pr >= 2:
                    dve.wait_ge(state_ready.sem, pr - 1)
                for part, (dst, src) in enumerate(((scan_re, rot_re), (scan_im, rot_im))):
                    if part:
                        after(rotated)
                    for w in range(2):
                        c = slice(256 * w, 256 * w + 256)
                        m = bc(mag_c[:, 2 * pr + w:2 * pr + w + 1], [P, 256])
                        ins = dve.tensor_tensor_scan(out=dst[:, b, c], data0=m, data1=src[:, c], initial=0.0, op0=ALU.mult, op1=ALU.add)
                link(dve, ins, scan_done)

            def skip(j):
                dve.wait_ge(y_part, 2 * j + 2)
                link(dve, dve.scalar_tensor_tensor(out=uT[:, j, :], in0=uT[:, j, :], scalar=dskip[:, j:j + 1],
                                                   in1=banks[6 + j % 2][:, 0:256], op0=ALU.mult, op1=ALU.add), y_free)

            def norm_rope(w):
                x4 = stag[w % 3].rearrange("p (i h n) -> p i h n", i=2, h=8)
                x3 = stag[w % 3].rearrange("p (h n) -> p h n", h=16)
                dve.wait_ge(sq_ready, w + 1)
                dve.tensor_reduce(hss, sq_tmp.rearrange("p (h n) -> p h n", h=16), AX.X, ALU.add).then_inc(hss_ready, 1)
                dve.wait_ge(hrs_ready, w + 1)
                link(dve, dve.reciprocal(hrs, hrs), dve1)
                link(dve, dve.tensor_tensor(x3, x3, bc(hrs.unsqueeze(2), [P, 16, 64]), ALU.mult), dve1)
                link(dve, dve.tensor_tensor(x3, x3, bc(qkw[:, w, :].unsqueeze(1), [P, 16, 64]), ALU.mult), dve1)
                t0, t1 = (ropt[:, n, :].rearrange("p (i h n) -> p i h n", i=2, h=8) for n in range(2))
                cos, sin = (bc(a.unsqueeze(2), [P, 2, 8, 8]) for a in (ropcos, ropsin))
                x1, x2 = x4[:, :, :, 0:8], x4[:, :, :, 8:16]
                t2, t3 = (sq_tmp[:, 128 * n:128 * n + 128].rearrange("p (i h n) -> p i h n", i=2, h=8) for n in range(2))
                mark(dve.tensor_tensor(t0, x1, cos, ALU.mult), dve1)
                mark(dve.tensor_tensor(t1, x2, sin, ALU.mult), dve1)
                mark(dve.tensor_tensor(t2, x2, cos, ALU.mult), dve1)
                link(dve, dve.tensor_tensor(t3, x1, sin, ALU.mult), dve1)
                mark(dve.tensor_tensor(x1, t0, t1, ALU.subtract), dve1)
                link(dve, dve.tensor_tensor(x2, t2, t3, ALU.add), qk_ready)

            for s in range(2):
                pj.after_read(dve, PJ_U + 6 + s)
            dve.wait_ge(rope_ready, 1)
            after(angle_sums(0))
            after(whole_turns(0))
            take_turns_off(0)
            dve.wait_ge(phase_ready.sem, 1)
            for pr in range(PAIRS):
                rotate_and_scan(pr)
                if pr >= 3 and pr % 2 == 1 and (pr - 3) // 2 < 6:
                    norm_rope((pr - 3) // 2)
                if pr >= 3 and pr % 2 == 1:
                    skip((pr - 3) // 2)
            skip(7)

            def mask_and_max(a, h, q, nk):
                dve.wait_ge(s_full, a + 1)
                if a >= 2:
                    dve.wait_ge(p_ready, a - 1)
                mask = C(f"mask{q}")
                for at in range(0, 3 * nk, 512):
                    n = min(512, 3 * nk - at)
                    ins = dve.scalar_tensor_tensor(out=s_sb[a % 2][:, at:at + n], in0=banks[4 + 2 * (a % 2) + at // 512][:, 0:n],
                                                   scalar=ATT_SCALE, in1=mask[:, at:at + n], op0=ALU.mult, op1=ALU.add)
                link(dve, ins, s_free)
                link(dve, dve.tensor_reduce(nmax[:, a:a + 1], s_sb[a % 2][:, 0:3 * nk], AX.X, ALU.max), dve1)
                link(dve, dve.tensor_scalar(nmax[:, a:a + 1], nmax[:, a:a + 1], -1.0, None, ALU.mult), m_ready)

            def normed_output(a, h, q):
                pj.to_read(dve, att_fill(a))
                link(dve, dve.reciprocal(rrec[:, a:a + 1], rsum[:, a:a + 1]), dve1)
                pj.emptied(dve.tensor_scalar(o_tok[:, q, 64 * h:64 * h + 64], pj.tile(att_fill(a))[:, 0:64], rrec[:, a:a + 1],
                                             None, ALU.mult), att_fill(a))

            dve.wait_ge(state_ready.sem, PAIRS)
            pieces = heads_blocks()
            mask_and_max(*pieces[0])
            for a, h, q, nk in pieces:
                if a + 1 < len(pieces):
                    mask_and_max(*pieces[a + 1])
                if a % 2 == 0:
                    m = a // 2
                    s = zs_fill(m)
                    dve.wait_ge(zt_ready, m + 1)
                    pj.emptied(dve.scalar_tensor_tensor(out=zs2[:, m, :], in0=zt[m % 2], scalar=1.0, in1=pj.tile(s)[:, 0:256],
                                                        op0=ALU.add, op1=ALU.mult), s)
                if a >= 1:
                    normed_output(*pieces[a - 1][0:3])
            normed_output(*pieces[15][0:3])
            for n in range(2):
                y = uT_[:, 1024 * n:1024 * n + 1024]
                link(dve, dve.tensor_tensor(gel[0], y, y, ALU.mult), dve1)
                link(dve, dve.tensor_scalar(gel[0], gel[0], 0.044715, 1.0, ALU.mult, ALU.add), dve1)
                dve.tensor_tensor(gel[1 + n], gel[0], y, ALU.mult).then_inc(gel_in, 1)
                dve.wait_ge(gel_in, n + 1)
            for n in range(2):
                y = uT_[:, 1024 * n:1024 * n + 1024]
                dve.wait_ge(gel_th, n + 1)
                dve.scalar_tensor_tensor(out=y, in0=gel[1 + n], scalar=1.0, in1=y, op0=ALU.add, op1=ALU.mult).then_inc(g_ready, 1)
            dve.wait_ge(g_ready, 2)
            for m in range(8):
                s = PJ_GLU + m
                if m < 2:
                    pj.after_read(dve, zs_fill(6 + m))
                pj.after_read(dve, s)
                link(dve, dve.scalar_tensor_tensor(out=gs[:, m, :], in0=zt[m % 2], scalar=1.0, in1=uT[:, m, :], op0=ALU.add,
                                                   op1=ALU.mult), dve1)
                dve.tensor_tensor(gs[:, m, :], gs[:, m, :], zs2[:, m, :], ALU.mult).then_inc(glu_used, 1)
            for n in range(2):
                s = PJ_ZA + n
                dve.wait_ge(th_za, n + 1)
                pj.emptied(dve.scalar_tensor_tensor(out=gate_b[:, n, :], in0=gate_a[:, n, :], scalar=1.0, in1=pj.tile(s)[:, :],
                                                    op0=ALU.add, op1=ALU.mult), s)
                pj.after_read(dve, s)
                dve.tensor_tensor(o_tok[:, n, :], o_tok[:, n, :], gate_b[:, n, :], ALU.mult).then_inc(oa_ready, 1)
            for n in range(4):
                s = PJ_SO + n
                i, c = n % 2, slice(512 * (n // 2), 512 * (n // 2) + 512)
                pj.to_read(dve, s)
                pj.after_read(dve, PJ_RS + n)
                pj.emptied(dve.scalar_tensor_tensor(out=m_tok[:, i, c], in0=th_s[:, i, c], scalar=1.0, in1=pj.tile(s)[:, :],
                                                    op0=ALU.add, op1=ALU.mult), s)
            for n in range(4):
                s = PJ_AO + n
                i, c = n % 2, slice(512 * (n // 2), 512 * (n // 2) + 512)
                pj.to_read(dve, s)
                pj.after_read(dve, PJ_RA + n)
                pj.after_read(dve, PJ_SO + n)
                pj.emptied(dve.scalar_tensor_tensor(out=th_a[:, i, c], in0=th_a[:, i, c], scalar=1.0, in1=pj.tile(s)[:, :],
                                                    op0=ALU.add, op1=ALU.mult), s)
                pj.after_read(dve, s)
                dve.scalar_tensor_tensor(out=m_tok[:, i, c], in0=th_a[:, i, c], scalar=4.0, in1=m_tok[:, i, c],
                                         op0=ALU.mult, op1=ALU.add).then_inc(m_done, 1)
            dve.wait_ge(xre_in, 16)
            for n in range(4):
                s = PJ_WO + n
                i, c = n % 2, slice(512 * (n // 2), 512 * (n // 2) + 512)
                pj.to_read(dve, s)
                pj.emptied(dve.tensor_tensor(xres[:, i, c], xres[:, i, c], pj.tile(s)[:, :], ALU.add), s)
            dve.wait_ge(sq2_done, 4)
            dve.tensor_tensor(ss2, ssq2[:, 0], ssq2[:, 1], ALU.add).then_inc(ss2_ready, 1)
            dve.wait_ge(root2_ready, 1)
            link(dve, dve.reciprocal(rstd2, rstd2), dve1)
            dve.tensor_tensor(diag2.rearrange("p (i n) -> p i n", i=2), bc(ident.unsqueeze(1), [P, 2, P]),
                              bc(rstd2.unsqueeze(2), [P, 2, P]), ALU.mult).then_inc(diag2_ready, 1)
            dve.wait_ge(xT2_full, 1)
            dve.wait_ge(mixw_in, 16)
            dve.wait_ge(rows2_ready, 1)
            for k in range(KD):
                ins = dve.scalar_tensor_tensor(out=hT[:, k, :], in0=banks[4 + k // 2][:, 256 * (k % 2):256 * (k % 2) + 256],
                                               scalar=mixw[:, k:k + 1], in1=rows2, op0=ALU.mult, op1=ALU.mult)
            ins.then_inc(hT2_ready, 1)
        scope.close()
        (PJ_HF, PJ_HQ, PJ_DQ, PJ_DK, PJ_HI, PJ_DV, PJ_HOG, PJ_O, PJ_DA, PJ_BHG, PJ_BDA, PJ_WOUT, PJ_END2) = (
            int(n) for n in PJ_END1 + np.cumsum([0, 4, 4, 2, 2, 2, 2, 2, 2, 16, 4, 4, 4]))

        def da_fill(a):
            return PJ_DA + 2 * a + 1

        def gate_fill(n):
            return PJ_DA + 2 * n

        TP_DQ, TP_DK, TP_KE, TP_ST, TP_HG, TP_DA, TP_DO, TP_M2, TP_R, TP_END2 = (
            int(n) for n in TP_END1 + np.cumsum([0, 2, 2, 2, 1, 2, 8, 2, 4, 4]))
        for name, s in ([("hf", PJ_HF + 3), ("hq", PJ_HQ + 3), ("dq", PJ_DQ + 1), ("dk", PJ_DK + 1), ("hi", PJ_HI + 1),
                         ("dv", PJ_DV + 1), ("hog", PJ_HOG + 1), ("bhg", PJ_BHG + 3), ("bda", PJ_BDA + 3)]
                        + [(f"ghg{n}", gate_fill(2 * n + 1)) for n in range(2)]
                        + [(f"gda{n}", gate_fill(2 * n + 5)) for n in range(2)]
                        + [(f"wout{n}", PJ_WOUT + 2 * n + 1) for n in range(2)]):
            last_fill[name] = s
        (e1_, e2_, e3_, e4_, hq_, hv_, ket_, o_, f_, k_, b_, d_, st_, state_, og_, hgT_, oda_, daT_) = carve(
            0, [1024] * 12 + [512, 1536] + [1024] * 4)
        by_head = lambda ap: ap.rearrange("p (h t) -> p h t", h=4)
        by_chunk = lambda ap: ap.rearrange("p (c t) -> p c t", c=16)
        by_tile = lambda ap: ap.rearrange("p (i n) -> p i n", i=2)
        f_t, k_t, b_t, qrel, krel, kend, qabs, hq_t = (by_head(a) for a in (f_, k_, b_, e1_, e2_, e3_, e4_, hq_))
        hi_tok, o_hg, og, oda = (by_tile(a) for a in (hv_, o_, og_, oda_))
        ke_tok = ket_.rearrange("p (i h n) -> p i h n", i=2, h=4)
        st = st_.rearrange("p (h i t) -> p h i t", h=4, i=2)
        state = state_.rearrange("p (c h n) -> p c h n", c=3, h=4)
        hgT, daT = (a.rearrange("p (k t) -> p k t", k=4) for a in (hgT_, daT_))
        th_hg = area[:, 8192:10240].rearrange("p (i n) -> p i n", i=2)
        th_da = area[:, 10240:12288].rearrange("p (i n) -> p i n", i=2)
        m2_, m2T_ = area[:, 12288:14336], area[:, 14336:16384]
        m2, m2T = m2_.rearrange("p (i n) -> p i n", i=2), m2T_.rearrange("p (k t) -> p k t", k=8)
        dstag = [work[:, 0:1024], work[:, 1024:2048]]
        dT_ = [work[:, 2048:3072], work[:, 3072:4096]]
        dT = [a.rearrange("p (h t) -> p h t", h=4) for a in dT_]
        dv_tok = work[:, 4096:5120].rearrange("p (i n) -> p i n", i=2)
        sq2 = work[:, 5120:6144]
        k_end_diff = xn[:, 1, :]
        ds_sb = [work[:, 5120 + 512 * n:5632 + 512 * n].rearrange("p (w n) -> p w n", w=2) for n in range(2)]
        dp_sb = [work[:, 6144 + 512 * n:6656 + 512 * n].rearrange("p (w n) -> p w n", w=2) for n in range(2)]
        da_sb = [work[:, 7168 + 256 * n:7424 + 256 * n] for n in range(2)]
        daT_sb = [work[:, 7680 + 256 * n:7936 + 256 * n] for n in range(2)]
        rt = [xn[:, 0, 256 * n:256 * n + 256] .rearrange("p (h n) -> p h n", h=8) for n in range(4)]

        lbm = small[:, 16:20]
        lb, lb1 = small[:, 20:24], small[:, 24:28]
        lamt = small[:, 668:796]
        lsum = small[:, 796:798]
        lam = small[:, 798:799]
        wr = small[:, 412:700].rearrange("p (k n) -> p k n", k=KD)
        biasr, gainc = small[:, 700:736], small[:, 736:744]
        ssq3, ss3, rstd3 = small[:, 916:920].rearrange("p (c i) -> p c i", c=2), small[:, 920:922], small[:, 922:924]
        dss, drs = small[:, 804:820], small[:, 820:836]
        oss, ors = small[:, 836:844], small[:, 844:852]
        eend = small[:, 852:868]
        dmax = small[:, 868:884]
        dsum = small[:, 884:900]
        drec = small[:, 900:916]

        act2, dve2 = Signal(sem("act_step2")), Signal(sem("dve_step2"))
        router_in, wr_ready, sq3_done, ss3_ready, var3_done, logits_full = (sem(s) for s in (
            "router_in", "wr_ready", "sq3_done", "ss3_ready", "var3_done", "logits_full"))
        lbe_in, lbe_ready, lam_in, lam_ready = sem("lbe_in"), sem("lbe_ready"), sem("lam_in"), sem("lam_ready")
        f_ready, ln_ready, diff_ready, exp_ready = sem("f_ready"), sem("ln_ready"), sem("diff_ready"), sem("exp_ready")
        dss_ready, drs_ready, dqk_ready = sem("dss_ready"), sem("drs_ready"), Signal(sem("dqk_ready"))
        prod_ready, th_hog = Signal(sem("prod_ready")), sem("th_hog")
        u_full, state_done, st_ready = sem("u_full"), Signal(sem("state_done")), sem("st_ready")
        oss_ready, ors_ready, og_ready = sem("oss_ready"), sem("ors_ready"), sem("og_ready")
        ds_full, ds_free, dm_ready, dp_ready, a_ready = (sem("ds_full"), Signal(sem("ds_free")), Signal(sem("dm_ready")),
                                                         sem("dp_ready"), Signal(sem("a_ready")))
        ods_ready, odr_ready, oda_ready, m2_done = sem("ods_ready"), sem("odr_ready"), sem("oda_ready"), sem("m2_done")

        def da_pieces():
            return [(2 * h + b, h, b, P * (b + 1)) for h in range(4) for b in range(2)]

        def turned_x(eng, s):
            c, i = divmod(s - TP_R, 2)
            dst, src = hT[:, 4 * c:4 * c + 4, P * i:P * i + P], tp.tile(s).rearrange("p (k t) -> p k t", k=4)
            tp.to_read(eng, s)
            tp.emptied(eng.tensor_copy(dst, src) if s == TP_R + 3 else eng.activation(dst, src, ACT.Copy), s)

        scope = ExitStack()
        block = scope.enter_context(nc.Block())

        @block.sync
        def _(sp):
            for n in range(n_units1 + SLOTS_BLOCKS, n_blocks):
                load_unit(sp, n)
            for m in (6, 7, 4, 5, 0, 1, 2, 3):
                if m >= 6:
                    tp.to_read(sp, TP_HG + 1)
                elif m >= 4:
                    pj.to_read(sp, da_fill(7))
                else:
                    pj.to_read(sp, last_fill[units[n_blocks - SLOTS_BLOCKS + m][0]])
                load_expert_unit(sp, m, 0)

        @block.gpsimd
        def _(pool):
            pool.wait_ge(lam_in, 1)

            def load_router(dst, src, **kw):
                pool.dma_start(dst, src, **kw).then_inc(router_in, 16)

            load_router(gainc, A["norm_moe_2"][0].rearrange("(k p) -> p k", p=P), allow_slow_non_contiguous=True)
            load_router(wr[:, :, 0:4], A["w_router_group_2"][0].rearrange("(k p) n -> p k n", p=P))
            load_router(wr[:, :, 4:36], A["w_router_expert_2"][0].rearrange("(k p) n -> p k n", p=P))
            load_router(biasr[:, 0:4], A["b_router_group_2"][0].partition_broadcast(P))
            load_router(biasr[:, 4:36], A["b_router_expert_2"][0].partition_broadcast(P))

        @block.scalar
        def _(act):
            act.wait_ge(lbe_in, 1)
            act.activation(lb2, lb2, ACT.Exp).then_inc(lbe_ready, 1)
            act.wait_ge(lam_in, 1)
            act.activation(lsum, lsum, ACT.Exp).then_inc(lam_ready, 1)
            for h in range(4):
                pj.to_read(act, PJ_HF + h)
                pj.emptied(act.activation(f_t[:, h, :], pj.tile(PJ_HF + h)[:, 0:256], ACT.Sigmoid), PJ_HF + h)
            for h in range(4):
                pj.to_read(act, PJ_HQ + h)
                pj.emptied(act.activation(hq_t[:, h, :], pj.tile(PJ_HQ + h)[:, 0:256], ACT.Copy), PJ_HQ + h)
            act.wait_ge(f_ready, 1)
            act.activation(b_, f_, ACT.Ln).then_inc(ln_ready, 1)

            def evacuate(dst, s):
                pj.to_read(act, s)
                pj.emptied(act.activation(dst, pj.tile(s)[:, :], ACT.Copy), s)

            for i in range(2):
                evacuate(dstag[0][:, 512 * i:512 * i + 512], PJ_DQ + i)
            act.wait_ge(diff_ready, 1)
            act.activation(e1_, d_, ACT.Exp)
            act.activation(e2_, d_, ACT.Exp, scale=-1.0)
            act.activation(e3_, k_end_diff, ACT.Exp, scale=-1.0)
            act.activation(eend, by_chunk(b_)[:, :, 63], ACT.Exp)
            act.activation(e4_, b_, ACT.Exp).then_inc(exp_ready, 1)
            for i in range(2):
                evacuate(dstag[1][:, 512 * i:512 * i + 512], PJ_DK + i)

            def head_sqrt(n):
                act.wait_ge(dss_ready, n + 1)
                act.activation(drs, dss, ACT.Sqrt, scale=1.0 / 64, bias=eps).then_inc(drs_ready, 1)

            def evacuate_turned(dst, first, n, scale=1.0):
                for s in range(first, first + n):
                    tp.to_read(act, s)
                    at = 512 * (s - first)
                    tp.emptied(act.activation(dst[:, at:at + 512], tp.tile(s)[:, :], ACT.Copy, scale=scale), s)

            head_sqrt(0)
            for i in range(2):
                evacuate(hi_tok[:, i, :], PJ_HI + i)
            evacuate_turned(dT_[0], TP_DQ, 2)
            head_sqrt(1)
            for i in range(2):
                evacuate(dv_tok[:, i, :], PJ_DV + i)
            evacuate_turned(dT_[1], TP_DK, 2)
            for i in range(2):
                pj.to_read(act, PJ_HOG + i)
                act.activation(og[:, i, :], pj.tile(PJ_HOG + i)[:, :], ACT.Tanh, scale=0.5).then_inc(th_hog, 1)
            evacuate_turned(ket_, TP_KE, 2)
            act.wait_ge(oss_ready, 1)
            act.activation(ors, oss, ACT.Sqrt, scale=1.0 / P, bias=eps).then_inc(ors_ready, 1)
            for a, h, q, nk in da_pieces():
                act.wait_ge(dm_ready.sem, a + 1)
                if a >= 2:
                    act.wait_ge(a_ready.sem, a - 1)
                for w in range(2):
                    n = 2 * a + w
                    ins = act.activation(dp_sb[a % 2][:, w, 0:nk], ds_sb[a % 2][:, w, 0:nk], ACT.Exp, bias=dmax[:, n:n + 1],
                                         accum_out=dsum[:, n:n + 1])
                ins.then_inc(dp_ready, 1)
                s = gate_fill(a)
                pj.to_read(act, s)
                dst = (th_hg, th_da)[a // 4][:, a % 2, 512 * (a % 4 // 2):512 * (a % 4 // 2) + 512]
                pj.emptied(act.activation(dst, pj.tile(s)[:, :], ACT.Tanh, scale=0.5), s)
                if a >= 2:
                    pj.to_read(act, da_fill(a - 2))
                if a == 0:
                    evacuate_turned(hgT_, TP_HG, 2, scale=0.5)
                tp.to_read(act, TP_DA + a)
                tp.emptied(act.activation(daT_sb[a % 2][:, 0:nk], tp.tile(TP_DA + a)[:, 0:nk], ACT.Copy), TP_DA + a)
            act.wait_ge(ods_ready, 1)
            act.activation(ors, oss, ACT.Sqrt, scale=1.0 / P, bias=eps).then_inc(odr_ready, 1)
            evacuate_turned(daT_, TP_DO, 2)
            evacuate_turned(m2T_, TP_M2, 4, scale=0.5)
            for n in range(4):
                i, c = n % 2, n // 2
                pj.after_read(act, PJ_WOUT + n)
                act.activation(xn[:, i, 512 * c:512 * c + 512], xres[:, i, 512 * c:512 * c + 512], ACT.Square,
                               accum_out=ssq3[:, c, i:i + 1]).then_inc(sq3_done, 1)
                if n == 1:
                    for i in range(2):
                        turned_x(act, TP_R + i)
            turned_x(act, TP_R + 2)
            act.wait_ge(ss3_ready, 1)
            act.activation(rstd3, ss3, ACT.Sqrt, scale=1.0 / D, bias=eps).then_inc(var3_done, 1)

        @block.tensor
        def _(pe):
            def turn(first, n_fills, blocks):
                for n in range(n_fills):
                    s = first + n
                    tp.to_fill(pe, s)
                    for c in range(4):
                        ins = pe.transpose(tp.tile(s)[:, P * c:P * c + P], blocks(4 * n + c), ident)
                    tp.filled(ins, s)

            def by_k(tok):
                return lambda n: tok[:, n % 2, P * (n // 2):P * (n // 2) + P]

            pe.wait_ge(hT2_ready, 1)
            for name, first in (("hf", PJ_HF), ("hq", PJ_HQ)):
                w = unit_ready(pe, name)
                for m in range(4):
                    pj.to_fill(pe, first + m)
                    pj.filled(project_t(pe, w, m, pj.tile(first + m)[:, 0:256], hT), first + m)

            def project_all(names, first, lhs):
                for n, name in enumerate(names):
                    w = unit_ready(pe, name)
                    for i in range(2):
                        s = first + 2 * n + i
                        pj.to_fill(pe, s)
                        pj.filled(project(pe, w, i, pj.tile(s)[:, :], lhs), s)

            project_all(["dq", "dk"], PJ_DQ, hT)
            project_all(["hi"], PJ_HI, hT)
            pe.wait_ge(dqk_ready.sem, 1)
            turn(TP_DQ, 2, by_k(dstag[0].rearrange("p (i n) -> p i n", i=2)))
            project_all(["dv"], PJ_DV, hT)
            pe.wait_ge(dqk_ready.sem, 2)
            turn(TP_DK, 2, by_k(dstag[1].rearrange("p (i n) -> p i n", i=2)))
            project_all(["hog"], PJ_HOG, hT)
            pe.wait_ge(prod_ready.sem, 4)
            turn(TP_KE, 2, lambda n: kend[:, n % 4, P * (n // 4):P * (n // 4) + P])
            tp.to_fill(pe, TP_ST)
            for c in range(4):
                half = slice(64 * (c % 2), 64 * (c % 2) + 64)
                for h in range(4):
                    at = 64 * (2 * h + c // 2)
                    ins = pe.matmul(tp.tile(TP_ST)[half, at:at + 64], krel[:, h, 64 * c:64 * c + 64], qrel[:, h, 64 * c:64 * c + 64],
                                    start=True, stop=True, tile_position=(0, 64 * (c % 2)))
            tp.filled(ins, TP_ST)
            for s in range(2):
                tp.after_read(pe, TP_KE + s)
                pj.after_read(pe, PJ_HI + s)
            for c in range(3):
                half, i = slice(64 * (c % 2), 64 * (c % 2) + 64), c // 2
                for h in range(4):
                    ins = pe.matmul(banks[4 + c][:, P * h:P * h + P], ke_tok[half, i, h, :], hi_tok[half, i, P * h:P * h + P],
                                    start=True, stop=True)
                ins.then_inc(u_full, 1)
            pe.wait_ge(st_ready, 1)
            for i in range(2):
                s = PJ_O + i
                pj.to_fill(pe, s)
                for c in (2 * i, 2 * i + 1):
                    half = slice(64 * (c % 2), 64 * (c % 2) + 64)
                    if c:
                        pe.wait_ge(state_done.sem, c)
                    for h in range(4):
                        dst = pj.tile(s)[half, P * h:P * h + P]
                        ins = pe.matmul(dst, st[half, h, i, :], hi_tok[half, i, P * h:P * h + P], start=True, stop=(c == 0))
                        if c:
                            ins = pe.matmul(dst, qabs[:, h, 64 * c:64 * c + 64], state[:, c - 1, h, :], start=False, stop=True,
                                            tile_position=(0, 64 * (c % 2)))
                pj.filled(ins, s)

            def da_scores(a, h, q, nk):
                if a == 0:
                    pe.wait_ge(state_done.sem, 3)
                elif a >= 2:
                    pe.wait_ge(ds_free.sem, a - 1)
                for w in range(2):
                    r = slice(64 * w, 64 * w + 64)
                    ins = pe.matmul(banks[4 + 2 * (a % 2) + w][:, 0:nk], dT[0][r, h, P * q:P * q + P], dT[1][r, h, 0:nk],
                                    start=True, stop=True)
                ins.then_inc(ds_full, 1)

            def da_turn(a, q):
                pe.wait_ge(a_ready.sem, a + 1)
                tp.to_fill(pe, TP_DA + a)
                for c in range(q + 1):
                    ins = pe.transpose(tp.tile(TP_DA + a)[:, P * c:P * c + P], da_sb[a % 2][:, P * c:P * c + P], ident)
                tp.filled(ins, TP_DA + a)

            def da_values(a, h, q):
                tp.after_read(pe, TP_DA + a)
                s = da_fill(a)
                pj.to_fill(pe, s)
                for c in range(q + 1):
                    ins = pe.matmul(pj.tile(s)[:, 0:P], daT_sb[a % 2][:, P * c:P * c + P], dv_tok[:, c, P * h:P * h + P],
                                    start=(c == 0), stop=(c == q))
                pj.filled(ins, s)

            for s in range(2):
                tp.after_read(pe, TP_DQ + s)
                tp.after_read(pe, TP_DK + s)
                pj.after_read(pe, PJ_DV + s)
            pieces = da_pieces()
            da_scores(*pieces[0])
            for a, h, q, nk in pieces:
                if a + 1 < len(pieces):
                    da_scores(*pieces[a + 1])
                if a >= 1:
                    da_values(*pieces[a - 1][0:3])
                w = unit_ready(pe, ("ghg0", "ghg1", "gda0", "gda1")[a // 2])
                s = gate_fill(a)
                pj.to_fill(pe, s)
                pj.filled(project(pe, w, a % 2, pj.tile(s)[:, :], hT), s)
                if a == 0:
                    pe.wait_ge(og_ready, 1)
                    turn(TP_HG, 2, by_k(og))
                da_turn(a, q)
            da_values(*pieces[7][0:3])
            for s in range(2):
                tp.after_read(pe, TP_HG + s)
            w = unit_ready(pe, "bhg")
            for n in range(4):
                s = PJ_BHG + n
                pj.to_fill(pe, s)
                pj.filled(project(pe, w, n % 2, pj.tile(s)[:, :], hgT, c0=512 * (n // 2)), s)
            pe.wait_ge(oda_ready, 1)
            turn(TP_DO, 2, by_k(oda))
            for s in range(2):
                tp.after_read(pe, TP_DO + s)
            w = unit_ready(pe, "bda")
            for n in range(4):
                s = PJ_BDA + n
                pj.to_fill(pe, s)
                pj.filled(project(pe, w, n % 2, pj.tile(s)[:, :], daT, c0=512 * (n // 2)), s)
            pe.wait_ge(m2_done, 4)
            turn(TP_M2, 4, by_k(m2))
            for s in range(2):
                tp.after_read(pe, TP_M2 + 2 + s)

            def turn_x(i, c):
                pj.after_read(pe, PJ_WOUT + 2 * c + i)
                turn(TP_R + 2 * c + i, 1, lambda n: xres[:, i, 512 * c + P * n:512 * c + P * n + P])

            for n in range(4):
                w = unit_ready(pe, f"wout{n // 2}")
                s = PJ_WOUT + n
                pj.to_fill(pe, s)
                pj.filled(project(pe, w, n % 2, pj.tile(s)[:, :], m2T), s)
                if n == 2:
                    turn_x(0, 0)
                    turn_x(1, 0)
            turn_x(0, 1)
            turn_x(1, 1)
            pe.wait_ge(wr_ready, 1)
            pe.wait_ge(ds_free.sem, 8)
            for i in range(2):
                tp.after_read(pe, TP_R + 2 + i)
                for k in range(KD):
                    ins = pe.matmul(banks[4][:, 36 * i:36 * i + 36], hT[:, k, P * i:P * i + P], wr[:, k, :],
                                    start=(k == 0), stop=(k == KD - 1))
            ins.then_inc(logits_full, 1)

        @block.vector
        def _(dve):
            dve.wait_ge(par2_in, 112)
            link(dve, dve.tensor_tensor(lbm, lb2[:, 0], lb2[:, 1], ALU.max), dve2)
            dve.tensor_tensor(lb2, lb2, bc(lbm.unsqueeze(1), [P, 2, 4]), ALU.subtract).then_inc(lbe_in, 1)
            for n in range(2):
                link(dve, dve.tensor_tensor(lamt[:, 64 * n:64 * n + 64], lamv[:, 2 * n], lamv[:, 2 * n + 1], ALU.mult), dve2)
            dve.tensor_reduce(lsum, lamt.rearrange("p (r n) -> p r n", r=2), AX.X, ALU.add).then_inc(lam_in, 1)
            dve.wait_ge(lbe_ready, 1)
            link(dve, dve.tensor_tensor(lbm, lb2[:, 0], lb2[:, 1], ALU.add), dve2)
            link(dve, dve.reciprocal(lbm, lbm), dve2)
            link(dve, dve.tensor_tensor(lb, lb2[:, 0], lbm, ALU.mult), dve2)
            link(dve, dve.tensor_scalar(lb1, lb, -1.0, 1.0, ALU.mult, ALU.add), dve2)
            dve.wait_ge(lam_ready, 1)
            link(dve, dve.tensor_tensor(lam, lsum[:, 0:1], lsum[:, 1:2], ALU.subtract), dve2)
            link(dve, dve.tensor_scalar(lam, lam, 0.8 - 0.6 * math.exp(-0.3 * 0), None, ALU.add), dve2)
            link(dve, dve.tensor_scalar(ogain, ogain, 1.0 - (0.8 - 0.6 * math.exp(-0.3 * 0)), None, ALU.mult), dve2)
            for h in range(4):
                pj.after_read(dve, PJ_HF + h)
                link(dve, dve.tensor_scalar(f_t[:, h, :], f_t[:, h, :], lb1[:, h:h + 1], lb[:, h:h + 1], ALU.mult, ALU.add), dve2)
            dve.tensor_scalar(k_, f_, -1.0, 1.0, ALU.mult, ALU.add).then_inc(f_ready, 1)
            dve.wait_ge(ln_ready, 1)
            for h in range(4):
                ins = dve.tensor_tensor_scan(out=f_t[:, h, :], data0=C("chunk0"), data1=b_t[:, h, :], initial=0.0,
                                             op0=ALU.mult, op1=ALU.add)
            link(dve, ins, dve2)
            link(dve, dve.tensor_copy(b_, f_), dve2)
            bv = by_chunk(b_)
            link(dve, dve.tensor_tensor(by_chunk(d_), bv, bc(bv[:, :, 31:32], [P, 16, 64]), ALU.subtract), dve2)
            dve.tensor_tensor(by_chunk(k_end_diff), bv, bc(bv[:, :, 63:64], [P, 16, 64]), ALU.subtract).then_inc(diff_ready, 1)

            def norm_rope2(n):
                x3 = dstag[n].rearrange("p (h n) -> p h n", h=16)
                for i in range(2):
                    pj.after_read(dve, (PJ_DQ, PJ_DK)[n] + i)
                link(dve, dve.tensor_tensor(sq2, dstag[n], dstag[n], ALU.mult), dve2)
                dve.tensor_reduce(dss, sq2.rearrange("p (h n) -> p h n", h=16), AX.X, ALU.add).then_inc(dss_ready, 1)
                dve.wait_ge(drs_ready, n + 1)
                link(dve, dve.reciprocal(drs, drs), dve2)
                link(dve, dve.tensor_tensor(x3, x3, bc(drs.unsqueeze(2), [P, 16, 64]), ALU.mult), dve2)
                link(dve, dve.tensor_tensor(x3, x3, bc(dgain[:, n].unsqueeze(1), [P, 16, 64]), ALU.mult), dve2)
                for i in range(2):
                    x1, x2 = x3[:, 8 * i:8 * i + 8, 0:32], x3[:, 8 * i:8 * i + 8, 32:64]
                    cos, sin = (bc(C(a)[:, 32 * i:32 * i + 32].unsqueeze(1), [P, 8, 32]) for a in ("cos2", "sin2"))
                    link(dve, dve.tensor_tensor(rt[0], x1, cos, ALU.mult), dve2)
                    link(dve, dve.tensor_tensor(rt[1], x2, sin, ALU.mult), dve2)
                    link(dve, dve.tensor_tensor(rt[2], x2, cos, ALU.mult), dve2)
                    link(dve, dve.tensor_tensor(rt[3], x1, sin, ALU.mult), dve2)
                    link(dve, dve.tensor_tensor(x1, rt[0], rt[1], ALU.subtract), dve2)
                    link(dve, dve.tensor_tensor(x2, rt[2], rt[3], ALU.add), dve2 if i == 0 else dqk_ready)

            norm_rope2(0)
            dve.wait_ge(exp_ready, 1)
            for s in range(2):
                pj.after_read(dve, PJ_HQ + 2 + s)
            for dst, src in ((e3_, k_), (e2_, k_), (e1_, hq_), (e4_, hq_)):
                link(dve, dve.tensor_tensor(dst, dst, src, ALU.mult), prod_ready)
            norm_rope2(1)
            for i in range(2):
                s = PJ_HOG + i
                dve.wait_ge(th_hog, i + 1)
                pj.emptied(dve.scalar_tensor_tensor(out=og[:, i, :], in0=og[:, i, :], scalar=1.0, in1=pj.tile(s)[:, :],
                                                    op0=ALU.add, op1=ALU.mult), s)
            tp.to_read(dve, TP_ST)
            tp.emptied(dve.tensor_scalar(st_, tp.tile(TP_ST)[:, :], 3e38, -3e38, ALU.min, ALU.max), TP_ST)
            tp.after_read(dve, TP_ST)
            sv = st_.rearrange("p (c t) -> p c t", c=8)
            dve.tensor_tensor(sv, sv, bc(C("tri64").unsqueeze(1), [P, 8, 64]), ALU.mult).then_inc(st_ready, 1)
            for c in range(3):
                dve.wait_ge(u_full, c + 1)
                if c == 0:
                    link(dve, dve.tensor_copy(state[:, 0].rearrange("p h n -> p (h n)"), banks[4]), state_done)
                    continue
                for h in range(4):
                    ins = dve.scalar_tensor_tensor(out=state[:, c, h, :], in0=state[:, c - 1, h, :],
                                                   scalar=eend[:, 4 * h + c:4 * h + c + 1], in1=banks[4 + c][:, P * h:P * h + P],
                                                   op0=ALU.mult, op1=ALU.add)
                link(dve, ins, state_done)

            def norm_out(o, sums_ready, roots_ready, gain):
                o3 = o.rearrange("p (h n) -> p h n", h=8)
                link(dve, dve.tensor_tensor(xn[:, 0, :], o, o, ALU.mult), dve2)
                dve.tensor_reduce(oss, xn[:, 0, :].rearrange("p (h n) -> p h n", h=8), AX.X, ALU.add).then_inc(sums_ready, 1)
                dve.wait_ge(roots_ready, 1)
                link(dve, dve.reciprocal(ors, ors), dve2)
                link(dve, dve.tensor_tensor(o3, o3, bc(ors.unsqueeze(2), [P, 8, P]), ALU.mult), dve2)
                return dve.tensor_tensor(o3, o3, bc(gain.unsqueeze(1), [P, 8, P]), ALU.mult)

            for i in range(2):
                s = PJ_O + i
                pj.to_read(dve, s)
                pj.emptied(dve.tensor_copy(o_hg[:, i, :], pj.tile(s)[:, :]), s)
            for i in range(2):
                pj.after_read(dve, PJ_O + i)
            link(dve, norm_out(o_, oss_ready, ors_ready, hgain), dve2)
            dve.tensor_tensor(og_, og_, o_, ALU.mult).then_inc(og_ready, 1)
            causal = [C("mask0")[:, 0:P], con[:, CONST_AT["none"][0]:CONST_AT["none"][0] + 2 * P]]

            def da_mask(a, h, q, nk):
                dve.wait_ge(ds_full, a + 1)
                if a >= 2:
                    dve.wait_ge(dp_ready, a - 1)
                for w in range(2):
                    ins = dve.scalar_tensor_tensor(out=ds_sb[a % 2][:, w, 0:nk], in0=banks[4 + 2 * (a % 2) + w][:, 0:nk], scalar=ATT_SCALE,
                                                   in1=causal[q], op0=ALU.mult, op1=ALU.add)
                link(dve, ins, ds_free)
                link(dve, dve.tensor_reduce(dmax[:, 2 * a:2 * a + 2], ds_sb[a % 2][:, :, 0:nk], AX.X, ALU.max), dve2)
                link(dve, dve.tensor_scalar(dmax[:, 2 * a:2 * a + 2], dmax[:, 2 * a:2 * a + 2], -1.0, None, ALU.mult), dm_ready)

            def da_combine(a, h, q, nk):
                dve.wait_ge(dp_ready, a + 1)
                if a >= 2:
                    tp.to_read(dve, TP_DA + a - 2)
                r = drec[:, 2 * a:2 * a + 2]
                link(dve, dve.reciprocal(r, dsum[:, 2 * a:2 * a + 2]), dve2)
                link(dve, dve.tensor_tensor(r[:, 1:2], r[:, 1:2], lam, ALU.mult), dve2)
                link(dve, dve.tensor_scalar(dp_sb[a % 2][:, 1, 0:nk], dp_sb[a % 2][:, 1, 0:nk], r[:, 1:2], None, ALU.mult), dve2)
                link(dve, dve.scalar_tensor_tensor(out=da_sb[a % 2][:, 0:nk], in0=dp_sb[a % 2][:, 0, 0:nk], scalar=r[:, 0:1],
                                                   in1=dp_sb[a % 2][:, 1, 0:nk], op0=ALU.mult, op1=ALU.subtract), a_ready)

            def da_out(a, h, q):
                s = da_fill(a)
                pj.to_read(dve, s)
                pj.emptied(dve.tensor_copy(oda[:, q, P * h:P * h + P], pj.tile(s)[:, 0:P]), s)

            pieces = da_pieces()
            da_mask(*pieces[0])
            for a, h, q, nk in pieces:
                if a + 1 < len(pieces):
                    da_mask(*pieces[a + 1])
                da_combine(a, h, q, nk)
                if a >= 1:
                    da_out(*pieces[a - 1][0:3])
            da_out(*pieces[7][0:3])
            for a in (6, 7):
                pj.after_read(dve, da_fill(a))
            norm_out(oda_, ods_ready, odr_ready, ogain).then_inc(oda_ready, 1)
            dve.wait_ge(router_in, 80)
            dve.tensor_tensor(wr, wr, bc(gainc.unsqueeze(2), [P, KD, 36]), ALU.mult).then_inc(wr_ready, 1)
            for n in range(4):
                s = PJ_BHG + n
                i, c = n % 2, slice(512 * (n // 2), 512 * (n // 2) + 512)
                pj.to_read(dve, s)
                pj.after_read(dve, gate_fill(n))
                pj.emptied(dve.scalar_tensor_tensor(out=m2[:, i, c], in0=th_hg[:, i, c], scalar=1.0, in1=pj.tile(s)[:, :],
                                                    op0=ALU.add, op1=ALU.mult), s)
            for n in range(4):
                s = PJ_BDA + n
                i, c = n % 2, slice(512 * (n // 2), 512 * (n // 2) + 512)
                pj.to_read(dve, s)
                pj.after_read(dve, gate_fill(4 + n))
                pj.after_read(dve, PJ_BHG + n)
                pj.emptied(dve.scalar_tensor_tensor(out=th_da[:, i, c], in0=th_da[:, i, c], scalar=1.0, in1=pj.tile(s)[:, :],
                                                    op0=ALU.add, op1=ALU.mult), s)
                pj.after_read(dve, s)
                dve.tensor_tensor(m2[:, i, c], m2[:, i, c], th_da[:, i, c], ALU.add).then_inc(m2_done, 1)
            for n in range(4):
                s = PJ_WOUT + n
                i, c = n % 2, slice(512 * (n // 2), 512 * (n // 2) + 512)
                pj.to_read(dve, s)
                pj.emptied(dve.tensor_tensor(xres[:, i, c], xres[:, i, c], pj.tile(s)[:, :], ALU.add), s)
            turned_x(dve, TP_R + 3)
            dve.wait_ge(sq3_done, 4)
            dve.tensor_tensor(ss3, ssq3[:, 0], ssq3[:, 1], ALU.add).then_inc(ss3_ready, 1)
        scope.close()

        gainr_, xg_, sel_, selw_, selT_, th_, act_, hid_, hidT_, y_, lg_ = carve(
            8192, [1024, 1024, 256, 256, 256, 512, 512, 512, 512, 1024, 72])
        xperm = xn[:, :, :].rearrange("p i (k q) -> p i k q", k=KD)
        xgT = xg_.rearrange("p (k s) -> p k s", k=KD)
        sel = sel_.rearrange("p (i q s) -> p i q s", i=2, q=4)
        selw = selw_.rearrange("p (i q s) -> p i q s", i=2, q=4)
        hid = hid_.rearrange("p (k q) -> p k q", k=4)
        hidT = hidT_.rearrange("p (k s) -> p k s", k=4)
        lg = lg_.rearrange("p (i n) -> p i n", i=2)
        lgg, lge = lg[:, :, 0:4], lg[:, :, 4:36].rearrange("p i (g e) -> p i g e", g=4)
        misc = area[:, 16384:18432]
        taken = [0]

        def tile3(*shape):
            n = int(np.prod(shape))
            ap = misc[:, taken[0]:taken[0] + n]
            taken[0] += n
            if len(shape) == 2:
                ap = ap.rearrange("p (a b) -> p a b", a=shape[0])
            elif len(shape) == 3:
                ap = ap.rearrange("p (a b c) -> p a b c", a=shape[0], b=shape[1])
            return ap

        gmax, gsum, gw, gtop = tile3(2), tile3(2), tile3(2), tile3(2)
        gexp, goh, gtmp = tile3(2, 4), tile3(2, 4), tile3(2, 4)
        prodg, eg, eg2 = tile3(2, 4, 8), tile3(2, 8), tile3(2, 8)
        m1, m2nd, top, ediff, p1, p2 = (tile3(2) for _ in range(6))
        oh1, oh2, t8, w8, s8 = (tile3(2, 8) for _ in range(5))
        wexp, aexp, place = tile3(2, 32), tile3(2, 32), tile3(2, 32)
        cmax, cnum = tile3(1), tile3(1)
        sweeps = sb("sweeps", [P, 1], I32)
        dummy = tile3(1)

        par3_in, rstd3_ready, x_scaled = sem("par3_in"), sem("rstd3_ready"), sem("x_scaled")
        scaled = hT[:, :, :].rearrange("p k t -> p (k t)").rearrange("p (i n) -> p i n", i=2)
        dve3, xn3_ready = Signal(sem("dve_step3")), sem("xn3_ready")
        exp_in3, exp_out3 = sem("exp_in3"), sem("exp_out3")
        chosen, places_full, sweeps_ready = sem("chosen"), sem("places_full"), sem("sweeps_ready")
        unit_used = sem("unit_used")
        (sel_ready, selw_ready, gather_full, selT_full, selT_ready, xg_low, xg_high, th_ready, act_ready, hid_ready, hidT_full,
         hidT_ready, y_low, y_high, combined, added, shifted, moe_done, out_done) = (sem(n) for n in (
             "sel_ready", "selw_ready", "gather_full", "selT_full", "selT_ready", "xg_low", "xg_high", "th_ready", "act_ready",
             "hid_ready", "hidT_full", "hidT_ready", "y_low", "y_high", "combined", "added", "shifted", "moe_done", "out_done"))

        def sweeps_over_groups(eng, group_body, before_sweep=None):
            with eng.Fori(0, N_GROUPS - 1, 2) as g:
                group_body(g, g, None, 0)
                group_body(g + 1, g + 1, None, 1)
            eng.wait_ge(sweeps_ready, 1)
            n = eng.value_load(sweeps[0:1, 0:1], min_val=1, max_val=T // SLOTS)
            with eng.If(n > 1):
                with eng.Fori(1, n) as s:
                    if before_sweep:
                        before_sweep(s)
                    with eng.Fori(0, N_GROUPS - 1, 2) as g:
                        group_body(s * N_GROUPS + g, g, s, 0)
                        group_body(s * N_GROUPS + g + 1, g + 1, s, 1)

        scope = ExitStack()
        block = scope.enter_context(nc.Block())

        @block.sync
        def _(sp):
            def load_pair(it, g, first=0):
                for m in range(first, 2 * UNITS):
                    sp.wait_ge(unit_used, it * UNITS + (m - NSEM_RING + 1))
                    load_expert_unit(sp, m % UNITS, g + m // UNITS, m // UNITS)

            load_pair(0, 0, first=NSEM_RING)
            with sp.Fori(2, N_GROUPS - 1, 2) as g:
                load_pair(g, g)
            sp.wait_ge(sweeps_ready, 1)
            n = sp.value_load(sweeps[0:1, 0:1], min_val=1, max_val=T // SLOTS)
            with sp.If(n > 1):
                with sp.Fori(1, n) as s:
                    with sp.Fori(0, N_GROUPS - 1, 2) as g:
                        load_pair(s * N_GROUPS + g, g)
            sp.wait_ge(moe_done, 1)
            sp.dma_start(out[0].rearrange("(i p) n -> p i n", p=P), xres[:, :, :]).then_inc(out_done, 16)
            sp.wait_ge(out_done, 16)

        @block.gpsimd
        def _(pool):
            def load(dst, src):
                pool.dma_start(dst, src).then_inc(par3_in, 16)

            load(gainr_, A["norm_moe_2"][0].partition_broadcast(P))
            pool.wait_ge(par3_in, 16)
            gq = gainr_.rearrange("p (q k) -> p q k", k=KD)
            for i in range(2):
                pool.wait_ge(x_scaled, i + 1)
                pool.tensor_tensor(xperm[:, i].rearrange("p k q -> p q k"), scaled[:, i, :].rearrange("p (q k) -> p q k", k=KD), gq,
                                   ALU.mult).then_inc(xn3_ready, 1)

        @block.scalar
        def _(act):
            act.wait_ge(rstd3_ready, 1)
            for i in range(2):
                act.activation(scaled[:, i, :], xres[:, i, :], ACT.Copy, scale=rstd3[:, i:i + 1]).then_inc(x_scaled, 1)
            act.wait_ge(exp_in3, 1)
            act.activation(gexp, gexp, ACT.Exp).then_inc(exp_out3, 1)
            act.wait_ge(exp_in3, 2)
            act.activation(ediff, ediff, ACT.Exp).then_inc(exp_out3, 1)

            def group(it, g, s, half):
                act.wait_ge(gather_full, it * 2 + 2)
                act.activation(xg_[:, 512:1024], banks[5], ACT.Copy).then_inc(xg_high, 1)
                act.wait_ge(selT_full, it + 1)
                act.activation(selT_, banks[6][:, 0:256], ACT.Copy).then_inc(selT_ready, 1)
                act.wait_ge(unit_used, it * UNITS + 4)
                act.activation(th_, banks[0], ACT.Tanh, scale=0.5).then_inc(th_ready, 1)
                act.wait_ge(hidT_full, it + 1)
                act.activation(hidT_, banks[7], ACT.Copy, scale=0.5).then_inc(hidT_ready, 1)
                act.wait_ge(unit_used, it * UNITS + 12)
                act.activation(y_[:, 512:1024], banks[3], ACT.Copy).then_inc(y_high, 1)

            sweeps_over_groups(act, group)

        @block.tensor
        def _(pe):
            pe.wait_ge(chosen, 1)
            up, ones = C("upper"), C("ones")
            pe.matmul(banks[5][:, 0:32], up, aexp[:, 0, :], start=True, stop=True)
            pe.matmul(banks[5][:, 32:64], ones, aexp[:, 0, :], start=True, stop=False)
            pe.matmul(banks[5][:, 32:64], up, aexp[:, 1, :], start=False, stop=True)
            pe.matmul(banks[5][:, 64:96], ones, aexp[:, 0, :], start=True, stop=False)
            pe.matmul(banks[5][:, 64:96], ones, aexp[:, 1, :], start=False, stop=True).then_inc(places_full, 1)

            pe.wait_ge(xn3_ready, 2)

            def expert_unit(it, half, m):
                u = half * UNITS + m
                s = u % NSEM_RING
                loads = 2 * UNITS // NSEM_RING
                pe.wait_ge(slot_loaded[s], (it - half) // 2 * (16 * loads) + 16 * (earlier_loads[s] + u // NSEM_RING + 1))
                return ring[:, s, :].rearrange("p (e n) -> p e n", e=GROUP_OF)

            def group(it, g, s, half):
                pe.wait_ge(sel_ready, it + 1)
                for k in range(KD):
                    for i in range(2):
                        ins = pe.matmul(banks[4 + k // 4][:, P * (k % 4):P * (k % 4) + P], xperm[:, i, k, :],
                                        sel_[:, P * i:P * i + P], start=(i == 0), stop=(i == 1))
                    if k % 4 == 3:
                        ins.then_inc(gather_full, 1)
                pe.wait_ge(selw_ready, it + 1)
                for i in range(2):
                    ins = pe.transpose(banks[6][:, P * i:P * i + P], selw_[:, P * i:P * i + P], ident)
                ins.then_inc(selT_full, 1)
                pe.wait_ge(xg_low, it + 1)
                pe.wait_ge(xg_high, it + 1)
                for m in range(8):
                    w = expert_unit(it, half, m)
                    for kk in range(2):
                        k = 2 * (m % 4) + kk
                        for q in range(GROUP_OF):
                            ins = pe.matmul(banks[m // 4][32 * q:32 * q + 32, :], xgT[:, k, 32 * q:32 * q + 32],
                                            w[:, q, FF * kk:FF * kk + FF], start=(k == 0), stop=(k == KD - 1), tile_position=(0, 32 * q))
                    ins.then_inc(unit_used, 1)
                pe.wait_ge(hid_ready, it + 1)
                for k in range(4):
                    ins = pe.transpose(banks[7][:, P * k:P * k + P], hid[:, k, :], ident)
                ins.then_inc(hidT_full, 1)
                pe.wait_ge(hidT_ready, it + 1)
                for m in range(8, 12):
                    w = expert_unit(it, half, m)
                    k = m - 8
                    for c in range(2):
                        for q in range(GROUP_OF):
                            ins = pe.matmul(banks[2 + c][32 * q:32 * q + 32, :], hidT[:, k, 32 * q:32 * q + 32],
                                            w[:, q, 512 * c:512 * c + 512], start=(k == 0), stop=(k == 3), tile_position=(0, 32 * q))
                    ins.then_inc(unit_used, 1)
                pe.wait_ge(selT_ready, it + 1)
                for n in range(4):
                    if n == 0:
                        pe.wait_ge(y_low, it + 1)
                    if n == 2:
                        pe.wait_ge(y_high, it + 1)
                        pe.wait_ge(added, it * 4 + 1)
                    if n == 3:
                        pe.wait_ge(added, it * 4 + 2)
                    pe.matmul(banks[6 + n % 2], selT_[:, P * (n % 2):P * (n % 2) + P], y_[:, 512 * (n // 2):512 * (n // 2) + 512],
                              start=True, stop=True).then_inc(combined, 1)
                pe.wait_ge(added, it * 4 + 4)

            sweeps_over_groups(pe, group)

        @block.vector
        def _(dve):
            dve.wait_ge(var3_done, 1)
            dve.reciprocal(rstd3, rstd3).then_inc(rstd3_ready, 1)
            dve.wait_ge(rstd3_ready, 1)
            step = lambda ins: link(dve, ins, dve3)
            b2 = lambda ap, n: bc(ap.unsqueeze(2), [P, 2, n])
            dve.wait_ge(logits_full, 1)
            for i in range(2):
                step(dve.scalar_tensor_tensor(out=lg[:, i], in0=banks[4][:, 36 * i:36 * i + 36], scalar=rstd3[:, i:i + 1], in1=biasr,
                                              op0=ALU.mult, op1=ALU.add))

            def first_largest(onehot, x, largest, rev, n, tmp):
                step(dve.tensor_tensor(tmp, x, b2(largest, n), ALU.is_equal))
                step(dve.tensor_tensor(tmp, tmp, bc(rev.unsqueeze(1), [P, 2, n]), ALU.mult))
                step(dve.tensor_reduce(top, tmp, AX.X, ALU.max))
                step(dve.tensor_tensor(onehot, tmp, b2(top, n), ALU.is_equal))

            step(dve.tensor_reduce(gmax, lgg, AX.X, ALU.max))
            dve.tensor_tensor(gexp, lgg, b2(gmax, 4), ALU.subtract).then_inc(exp_in3, 1)
            first_largest(goh, lgg, gmax, C("rev4"), 4, gtmp)
            dve.wait_ge(exp_out3, 1)
            step(dve.tensor_reduce(gsum, gexp, AX.X, ALU.add))
            step(dve.reciprocal(gw, gsum))
            for i in range(2):
                step(dve.tensor_tensor(prodg[:, i], lge[:, i], bc(goh[:, i].unsqueeze(2), [P, 4, 8]), ALU.mult))
                step(dve.tensor_reduce(eg[:, i], prodg[:, i].rearrange("p g e -> p e g"), AX.X, ALU.add))
            step(dve.tensor_reduce(m1, eg, AX.X, ALU.max))
            first_largest(oh1, eg, m1, C("rev8"), 8, t8)
            step(dve.scalar_tensor_tensor(out=eg2, in0=oh1, scalar=NEG, in1=eg, op0=ALU.mult, op1=ALU.add))
            step(dve.tensor_reduce(m2nd, eg2, AX.X, ALU.max))
            first_largest(oh2, eg2, m2nd, C("rev8"), 8, t8)
            dve.tensor_tensor(ediff, m2nd, m1, ALU.subtract).then_inc(exp_in3, 1)
            dve.wait_ge(exp_out3, 2)
            step(dve.tensor_scalar(p1, ediff, 1.0, None, ALU.add))
            step(dve.reciprocal(p1, p1))
            step(dve.tensor_tensor(p1, p1, gw, ALU.mult))
            step(dve.tensor_tensor(p2, p1, ediff, ALU.mult))
            step(dve.tensor_tensor(s8, oh1, oh2, ALU.add))
            step(dve.tensor_tensor(w8, oh1, b2(p1, 8), ALU.mult))
            step(dve.tensor_tensor(t8, oh2, b2(p2, 8), ALU.mult))
            step(dve.tensor_tensor(w8, w8, t8, ALU.add))
            for dst, src in ((wexp, w8), (aexp, s8)):
                for i in range(2):
                    step(dve.tensor_tensor(dst[:, i].rearrange("p (g e) -> p g e", g=4), bc(src[:, i].unsqueeze(1), [P, 4, 8]),
                                           bc(goh[:, i].unsqueeze(2), [P, 4, 8]), ALU.mult))
            dve.tensor_copy(dummy, p1[:, 0:1]).then_inc(chosen, 1)
            dve.wait_ge(places_full, 1)
            pl = banks[5][:, 0:64].rearrange("p (i n) -> p i n", i=2)
            step(dve.tensor_tensor(place, aexp, pl, ALU.mult))
            step(dve.tensor_scalar(place, place, 1.0, None, ALU.subtract))
            step(dve.tensor_reduce(cmax, banks[5][:, 64:96], AX.X, ALU.max))
            step(dve.tensor_scalar(cnum, cmax, 1.0 / SLOTS, (SLOTS - 1) / SLOTS - (SLOTS - 1) / (2 * SLOTS), ALU.mult, ALU.add))
            step(dve.tensor_scalar(cnum, cnum, ROUND, ROUND, ALU.add, ALU.subtract))
            dve.tensor_copy(sweeps[:, :], cnum).then_inc(sweeps_ready, 1)

            def group(it, g, s, half):
                four = bass.ds(g * GROUP_OF, GROUP_OF)
                slots = C("iota")[:, 0:SLOTS]
                if s is not None:
                    dve.wait_ge(shifted, s)
                for i in range(2):
                    ins = dve.tensor_tensor(sel[:, i], bc(slots.unsqueeze(1), [P, 4, SLOTS]),
                                            bc(place[:, i, four].unsqueeze(2), [P, 4, SLOTS]), ALU.is_equal)
                ins.then_inc(sel_ready, 1)
                dve.wait_ge(sel_ready, it + 1)
                for i in range(2):
                    ins = dve.tensor_tensor(selw[:, i], sel[:, i], bc(wexp[:, i, four].unsqueeze(2), [P, 4, SLOTS]), ALU.mult)
                ins.then_inc(selw_ready, 1)
                dve.wait_ge(gather_full, it * 2 + 1)
                dve.tensor_copy(xg_[:, 0:512], banks[4]).then_inc(xg_low, 1)
                dve.wait_ge(th_ready, it + 1)
                dve.scalar_tensor_tensor(out=act_, in0=th_, scalar=1.0, in1=banks[0], op0=ALU.add, op1=ALU.mult).then_inc(act_ready, 1)
                dve.wait_ge(act_ready, it + 1)
                dve.wait_ge(unit_used, it * UNITS + 8)
                dve.tensor_tensor(hid.rearrange("p k q -> p q k"), act_.rearrange("p (q k) -> p q k", k=4),
                                  banks[1].rearrange("p (q k) -> p q k", k=4), ALU.mult).then_inc(hid_ready, 1)
                dve.wait_ge(unit_used, it * UNITS + 12)
                dve.tensor_copy(y_[:, 0:512], banks[2]).then_inc(y_low, 1)
                for n in range(4):
                    dst = xres[:, n % 2, 512 * (n // 2):512 * (n // 2) + 512]
                    dve.wait_ge(combined, it * 4 + (n + 1))
                    dve.tensor_tensor(dst, dst, banks[6 + n % 2], ALU.add).then_inc(added, 1)
                dve.wait_ge(added, it * 4 + 4)

            def next_places(s):
                dve.tensor_scalar(place, place, float(SLOTS), None, ALU.subtract).then_inc(shifted, 1)

            dve.wait_ge(sweeps_ready, 1)
            sweeps_over_groups(dve, group, next_places)
            dve.tensor_copy(dummy, p1[:, 0:1]).then_inc(moe_done, 1)
        scope.close()


def kernel(**inputs):
    import concourse.bacc as bacc
    from concourse.bass_utils import run_bass_kernel_spmd

    nc = bacc.Bacc("TRN2", target_bir_lowering=False, num_devices=1)
    arrays, aps = {}, {}
    for name in INPUTS:
        a = np.ascontiguousarray(inputs[name])
        arrays["in_" + name] = a
        aps[name] = nc.dram_tensor("in_" + name, a.shape, mybir.dt.from_np(a.dtype), kind="ExternalInput").ap()
    arrays["in_constants"] = constants()
    aps["constants"] = nc.dram_tensor("in_constants", (P, NCONST), F32, kind="ExternalInput").ap()
    out = nc.dram_tensor("out_0", (1, T, D), F32, kind="ExternalOutput").ap()
    build(nc, aps, out)
    r = run_bass_kernel_spmd(nc, [arrays], core_ids=[0])
    return r.results[0]["out_0"]
```
